# Optimizing a Trainium2 kernel written in Bass

```python
import math
import jax, jax.numpy as jnp
from jax import lax
import numpy as np

D_MODEL = 1024
BATCH = 1
SEQ = 512
DEPTH = 2

CHUNK = 64
N_HEADS = 8
HEAD_DIM = 64
ATTN_W = N_HEADS * HEAD_DIM
KV_DIM = HEAD_DIM
IDX_HEADS = 4
IDX_DIM = 64
TOPK_MAX = 256
Q_BLOCK = 128
SSM_W = D_MODEL - ATTN_W
SSM_GROUP = 16
SSM_GROUPS = SSM_W // SSM_GROUP
SSM_STATE = 64
SCAN_BLOCK = 128
DT_MIN = 1e-3
DT_MAX = 1e-1
ROPE_THETA = 500000.0
ROT_DIM = HEAD_DIM // 4
D_FF = 2816
MIX_W = ATTN_W + SSM_W
EPS = 1e-6
N_MOD = 9
IN_COLS = ATTN_W + 2 * KV_DIM + IDX_HEADS * IDX_DIM + IDX_DIM + IDX_HEADS + SSM_W
IN_SPLITS = (
    ATTN_W,
    ATTN_W + KV_DIM,
    ATTN_W + 2 * KV_DIM,
    ATTN_W + 2 * KV_DIM + IDX_HEADS * IDX_DIM,
    ATTN_W + 2 * KV_DIM + IDX_HEADS * IDX_DIM + IDX_DIM,
    ATTN_W + 2 * KV_DIM + IDX_HEADS * IDX_DIM + IDX_DIM + IDX_HEADS,
)

kernel_name = 'hybrid_dsa_s5_macaron_adaln'

def rms_norm(x, g):
    xf = x.astype(jnp.float32)
    y = xf * lax.rsqrt(jnp.mean(xf * xf, axis=-1, keepdims=True) + EPS)
    return (y * g.astype(jnp.float32)).astype(x.dtype)

def modulate(h, shift, scale):
    return h * (1.0 + scale[:, None, :]) + shift[:, None, :]

def swiglu(h, w1, w3, w2):
    return (jax.nn.silu(h @ w1) * (h @ w3)) @ w2

def rope_tables(positions):
    inv_freq = 1.0 / (ROPE_THETA ** (jnp.arange(0, ROT_DIM, 2, dtype=jnp.float32) / ROT_DIM))
    ang = positions.astype(jnp.float32)[..., None] * inv_freq
    return jnp.cos(ang), jnp.sin(ang)

def apply_partial_rope(t, cos, sin):
    half = ROT_DIM // 2
    tf = t.astype(jnp.float32)
    t1 = tf[..., :half]
    t2 = tf[..., half:ROT_DIM]
    cs = cos[:, :, None, :]
    sn = sin[:, :, None, :]
    out = jnp.concatenate([t1 * cs - t2 * sn, t1 * sn + t2 * cs, tf[..., ROT_DIM:]], axis=-1)
    return out.astype(t.dtype)

def dsa_attention(q, k, v, qi, ki, wi):
    bsz, seq = q.shape[0], q.shape[1]
    topk = min(TOPK_MAX, seq // 4)
    nb = seq // Q_BLOCK
    key_chunk = jnp.arange(seq) // CHUNK
    idx_scale = IDX_DIM ** -0.5 * IDX_HEADS ** -0.5
    att_scale = HEAD_DIM ** -0.5
    gather = jax.vmap(lambda t, i: t[i])

    def to_blocks(t):
        return jnp.moveaxis(t.reshape((bsz, nb, Q_BLOCK) + t.shape[2:]), 1, 0)

    def block_fn(args):
        start, qb, qib, wb = args
        q_chunk = (start + jnp.arange(Q_BLOCK)) // CHUNK
        rel = jax.nn.relu(jnp.einsum('bqhd,bsd->bqhs', qib, ki, preferred_element_type=jnp.float32))
        score = jnp.einsum('bqhs,bqh->bqs', rel, wb.astype(jnp.float32)) * idx_scale
        admissible = key_chunk[None, :] <= q_chunk[:, None]
        score = jnp.where(admissible[None], score, -jnp.inf)
        vals, idx = lax.top_k(score, topk)
        k_sel = gather(k, idx)
        v_sel = gather(v, idx)
        logits = jnp.einsum('bqhd,bqkd->bqhk', qb, k_sel, preferred_element_type=jnp.float32) * att_scale
        logits = jnp.where(jnp.isfinite(vals)[:, :, None, :], logits, -jnp.inf)
        p = jax.nn.softmax(logits, axis=-1)
        return jnp.einsum('bqhk,bqkd->bqhd', p.astype(v_sel.dtype), v_sel)

    starts = jnp.arange(nb, dtype=jnp.int32) * Q_BLOCK
    out = lax.map(block_fn, (starts, to_blocks(q), to_blocks(qi), to_blocks(wi)))
    out = jnp.moveaxis(out, 0, 1).reshape(bsz, seq, N_HEADS * HEAD_DIM)
    return out

def s5_ssm(u, a_re, a_im, log_dt, b_re, b_im, c_re, c_im, d_skip):
    bsz, seq, _ = u.shape
    nb = seq // SCAN_BLOCK
    uf = u.astype(jnp.float32).reshape(bsz, nb, SCAN_BLOCK, SSM_GROUPS, SSM_GROUP)
    uf = uf.transpose(1, 2, 0, 3, 4)
    a = lax.complex(a_re.astype(jnp.float32), a_im.astype(jnp.float32))
    dt = jnp.exp(log_dt.astype(jnp.float32))[:, None]
    a_bar = jnp.exp(a * dt)
    b_bar = ((a_bar - 1.0) / a)[:, :, None] * lax.complex(b_re.astype(jnp.float32), b_im.astype(jnp.float32))
    c_mat = lax.complex(c_re.astype(jnp.float32), c_im.astype(jnp.float32))
    d_f = d_skip.astype(jnp.float32)
    a_elems = jnp.broadcast_to(a_bar, (SCAN_BLOCK, 1, SSM_GROUPS, SSM_STATE))

    def combine(e1, e2):
        a1, b1 = e1
        a2, b2 = e2
        return a1 * a2, a2 * b1 + b2

    def step(h, ub):
        bu = jnp.einsum('gpc,sbgc->sbgp', b_bar, ub.astype(jnp.complex64))
        a_cum, b_scan = lax.associative_scan(combine, (a_elems, bu), axis=0)
        states = a_cum * h[None] + b_scan
        y = jnp.einsum('gcp,sbgp->sbgc', c_mat, states).real + d_f * ub
        return states[-1], y

    h0 = jnp.zeros((bsz, SSM_GROUPS, SSM_STATE), jnp.complex64)
    _, ys = lax.scan(step, h0, uf)
    return ys.transpose(2, 0, 1, 3, 4).reshape(bsz, seq, SSM_W).astype(u.dtype)

def hybrid_mixer(h, cos, sin, w_in, w_out, attn_gain, ssm_gain, a_re, a_im, log_dt,
                 b_re, b_im, c_re, c_im, d_skip, glu_w, glu_b):
    bsz, seq, _ = h.shape
    proj = h @ w_in
    q, k, v, qi, ki, wi, u = jnp.split(proj, IN_SPLITS, axis=-1)
    q = apply_partial_rope(q.reshape(bsz, seq, N_HEADS, HEAD_DIM), cos, sin)
    k = apply_partial_rope(k[:, :, None, :], cos, sin)[:, :, 0, :]
    qi = apply_partial_rope(qi.reshape(bsz, seq, IDX_HEADS, IDX_DIM), cos, sin)
    ki = apply_partial_rope(ki[:, :, None, :], cos, sin)[:, :, 0, :]
    attn = dsa_attention(q, k, v, qi, ki, wi)
    y = s5_ssm(u, a_re, a_im, log_dt, b_re, b_im, c_re, c_im, d_skip)
    y = jax.nn.gelu(y)
    y = y * jax.nn.sigmoid(y @ glu_w + glu_b)
    mixed = jnp.concatenate([rms_norm(attn, attn_gain), rms_norm(y, ssm_gain)], axis=-1)
    return mixed @ w_out

def setup_inputs(seed: int = 0) -> dict:
    key = jax.random.key(seed)
    ks = jax.random.split(key, 32)
    f32 = jnp.float32

    def nrm(k, shape, scale):
        return jax.random.normal(k, shape, f32) * scale

    x = nrm(ks[0], (BATCH, SEQ, D_MODEL), 1.0)
    c = nrm(ks[1], (BATCH, D_MODEL), 1.0)
    offsets = jax.random.randint(ks[2], (BATCH,), 0, 64, dtype=jnp.int32) * CHUNK
    positions = jnp.arange(SEQ, dtype=jnp.int32)[None, :] + offsets[:, None]
    mod_w = nrm(ks[3], (DEPTH, D_MODEL, N_MOD * D_MODEL), 0.5 * D_MODEL ** -0.5)
    mod_b = nrm(ks[4], (DEPTH, N_MOD * D_MODEL), 0.02)
    norm_g = 1.0 + nrm(ks[5], (DEPTH, 3, D_MODEL), 0.02)
    ffn1_w1 = nrm(ks[6], (DEPTH, D_MODEL, D_FF), D_MODEL ** -0.5)
    ffn1_w3 = nrm(ks[7], (DEPTH, D_MODEL, D_FF), D_MODEL ** -0.5)
    ffn1_w2 = nrm(ks[8], (DEPTH, D_FF, D_MODEL), D_FF ** -0.5)
    ffn2_w1 = nrm(ks[9], (DEPTH, D_MODEL, D_FF), D_MODEL ** -0.5)
    ffn2_w3 = nrm(ks[10], (DEPTH, D_MODEL, D_FF), D_MODEL ** -0.5)
    ffn2_w2 = nrm(ks[11], (DEPTH, D_FF, D_MODEL), D_FF ** -0.5)
    w_in = nrm(ks[12], (DEPTH, D_MODEL, IN_COLS), D_MODEL ** -0.5)
    w_out = nrm(ks[13], (DEPTH, MIX_W, D_MODEL), MIX_W ** -0.5)
    attn_gain = 1.0 + nrm(ks[14], (DEPTH, ATTN_W), 0.02)
    ssm_gain = 1.0 + nrm(ks[15], (DEPTH, SSM_W), 0.02)
    gp = (DEPTH, SSM_GROUPS, SSM_STATE)
    ssm_a_re = -0.5 * jnp.exp(nrm(ks[16], gp, 0.02))
    ssm_a_im = math.pi * jnp.arange(SSM_STATE, dtype=f32)[None, None, :] + nrm(ks[17], gp, 0.01)
    ssm_log_dt = jax.random.uniform(ks[18], (DEPTH, SSM_GROUPS), f32, math.log(DT_MIN), math.log(DT_MAX))
    ssm_b_re = nrm(ks[19], (DEPTH, SSM_GROUPS, SSM_STATE, SSM_GROUP), (2 * SSM_GROUP) ** -0.5)
    ssm_b_im = nrm(ks[20], (DEPTH, SSM_GROUPS, SSM_STATE, SSM_GROUP), (2 * SSM_GROUP) ** -0.5)
    ssm_c_re = nrm(ks[21], (DEPTH, SSM_GROUPS, SSM_GROUP, SSM_STATE), SSM_STATE ** -0.5)
    ssm_c_im = nrm(ks[22], (DEPTH, SSM_GROUPS, SSM_GROUP, SSM_STATE), SSM_STATE ** -0.5)
    ssm_d = nrm(ks[23], (DEPTH, SSM_GROUPS, SSM_GROUP), 1.0)
    glu_w = nrm(ks[24], (DEPTH, SSM_W, SSM_W), SSM_W ** -0.5)
    glu_b = nrm(ks[25], (DEPTH, SSM_W), 0.02)
    final_g = 1.0 + nrm(ks[26], (D_MODEL,), 0.02)
    return {
        'x': x, 'c': c, 'positions': positions,
        'mod_w': mod_w, 'mod_b': mod_b, 'norm_g': norm_g,
        'ffn1_w1': ffn1_w1, 'ffn1_w3': ffn1_w3, 'ffn1_w2': ffn1_w2,
        'ffn2_w1': ffn2_w1, 'ffn2_w3': ffn2_w3, 'ffn2_w2': ffn2_w2,
        'w_in': w_in, 'w_out': w_out, 'attn_gain': attn_gain, 'ssm_gain': ssm_gain,
        'ssm_a_re': ssm_a_re, 'ssm_a_im': ssm_a_im, 'ssm_log_dt': ssm_log_dt,
        'ssm_b_re': ssm_b_re, 'ssm_b_im': ssm_b_im, 'ssm_c_re': ssm_c_re, 'ssm_c_im': ssm_c_im,
        'ssm_d': ssm_d, 'glu_w': glu_w, 'glu_b': glu_b, 'final_g': final_g,
    }

def reference(x, c, positions, mod_w, mod_b, norm_g, ffn1_w1, ffn1_w3, ffn1_w2,
              ffn2_w1, ffn2_w3, ffn2_w2, w_in, w_out, attn_gain, ssm_gain,
              ssm_a_re, ssm_a_im, ssm_log_dt, ssm_b_re, ssm_b_im, ssm_c_re, ssm_c_im,
              ssm_d, glu_w, glu_b, final_g):
    cos, sin = rope_tables(positions)
    for l in range(DEPTH):
        mod = jax.nn.silu(c) @ mod_w[l] + mod_b[l]
        sh1, sc1, g1, sh2, sc2, g2, sh3, sc3, g3 = jnp.split(mod, N_MOD, axis=-1)
        h = modulate(rms_norm(x, norm_g[l, 0]), sh1, sc1)
        x = x + 0.5 * g1[:, None, :] * swiglu(h, ffn1_w1[l], ffn1_w3[l], ffn1_w2[l])
        h = modulate(rms_norm(x, norm_g[l, 1]), sh2, sc2)
        x = x + g2[:, None, :] * hybrid_mixer(
            h, cos, sin, w_in[l], w_out[l], attn_gain[l], ssm_gain[l],
            ssm_a_re[l], ssm_a_im[l], ssm_log_dt[l], ssm_b_re[l], ssm_b_im[l],
            ssm_c_re[l], ssm_c_im[l], ssm_d[l], glu_w[l], glu_b[l])
        h = modulate(rms_norm(x, norm_g[l, 2]), sh3, sc3)
        x = x + 0.5 * g3[:, None, :] * swiglu(h, ffn2_w1[l], ffn2_w3[l], ffn2_w2[l])
    return rms_norm(x, final_g)


_drawn_inputs = setup_inputs


def setup_inputs(seed=0):
    import zlib

    import numpy as np

    out = dict(_drawn_inputs(seed))
    spreads = {}
    factors = {'norm_g': 2.748,
     'attn_gain': 7.405,
     'ssm_gain': 7.309,
     'ssm_a_re': 8.0,
     'glu_b': 8.0,
     'final_g': 2.809}
    for name, (base, spread) in spreads.items():
        noise = np.random.default_rng([zlib.crc32(name.encode()), seed]).standard_normal(out[name].shape)
        drawn = base * np.exp(spread * noise) if base else spread * noise
        out[name] = __import__('jax').numpy.asarray(drawn.astype(out[name].dtype))
    for name, factor in factors.items():
        out[name] = (out[name] * factor).astype(out[name].dtype)
    return out
```

```python
from contextlib import ExitStack

import numpy as np

import concourse.bass as bass
from concourse import mybir

F32 = mybir.dt.float32
F32R = mybir.dt.float32r
I32 = mybir.dt.int32
ALU = mybir.AluOpType
ACT = mybir.ActivationFunctionType
ds = bass.ds

P = 128
DEPTH = 2
D = 1024
KT = D // P
SEQ = 512
QB = SEQ // P
F = 2816
FT = F // P
HEADS = 8
HD = 64
AT = HEADS * HD // P
IDX_HEADS = 4
TOPK = 128
SW = 512
ST = SW // P
G = 32
GC = 16
NS = 64
L = 8
J = SEQ // L
GI = 4
N_MOD = 9
EPS = 1e-6
ATT_SCALE = HD ** -0.5
IDX_SCALE = HD ** -0.5 * IDX_HEADS ** -0.5
ROT = HD // 4
INV_FREQ = (1, 0.193922758, 0.0376060307, 0.00729266508, 0.00141421345,
            0.000274248188, 5.31829573e-05, 1.03133852e-05)
COL_K, COL_KI, COL_QI, COL_U = 512, 896, 640, 964
NEG = -1.0e30
INADM = -3.0e38
TAKEN = -3.4e38
TWO_PI_A, TWO_PI_B, TWO_PI_C = 6.28125, 0.0019350051879882812, 3.019915981956753e-07
INV_2PI = 0.15915494309189535
ROUND = 12582912.0
HALF_PI = 1.5707963267948966

RING = 4
AHEAD = 2
DOWN_K = (8, 8, 6)
FFN_CHUNKS = 2 * FT + KT * len(DOWN_K)
MIX_CHUNKS = 8 + ST + ST + KT
FFN_BASE = (0, FFN_CHUNKS + MIX_CHUNKS)
MIX_BASE = FFN_CHUNKS
LAYER_CHUNKS = 2 * FFN_CHUNKS + MIX_CHUNKS
assert LAYER_CHUNKS % RING == 0
A_UNROLL = 4
A_TURNS = (FT - 2) // A_UNROLL
MOD_RING = 2
DVE_STEPS, POOL_STEPS = 304, 208

C_ID, C_SWAP, C_RK, C_SRK, C_RKI, C_SRKI = (i * P for i in range(6))
C_COLS = 6 * P


def shape_constants():
    t = np.zeros((P, 6 * P + 4), np.float32)
    m = np.arange(P)
    d = m % HD
    other = np.where(d < ROT // 2, m + ROT // 2, np.where(d < ROT, m - ROT // 2, m))
    rot = d < ROT
    t[m, C_ID + m] = 1.0
    t[other[rot], C_SWAP + m[rot]] = 1.0
    t[d, C_RK + m] = 1.0
    t[(other % HD)[rot], C_SRK + m[rot]] = 1.0
    t[d + HD, C_RKI + m] = 1.0
    t[(other % HD + HD)[rot], C_SRKI + m[rot]] = 1.0
    freq = np.array(INV_FREQ, np.float32)
    t[:, C_COLS] = np.where(rot, freq[d % (ROT // 2)], 0.0)
    t[:, C_COLS + 1] = np.where(rot, np.where(d < ROT // 2, -1.0, 1.0), 0.0)
    t[:, C_COLS + 2] = rot
    t[:, C_COLS + 3] = ~rot
    return t


class Signal:

    def __init__(self, sem, per, start=0):
        self.sem, self.per, self.start = sem, per, start

    def after(self, layer, k):
        return layer * self.per + (self.start + k + 1)


class Chain:

    def __init__(self, eng, sem, layer, per):
        self.eng, self.sem, self.base, self.n = eng, sem, layer * per, 0

    def __call__(self, *instructions):
        for i in instructions:
            i.then_inc(self.sem, 1)
            self.n += 1
        self.eng.wait_ge(self.sem, self.base + self.n)


def trunk(nc, a):
    ctx = ExitStack()
    with ctx:
        def sb(name, shape, dt=F32, at=None):
            return (at or ctx).enter_context(nc.sbuf_tensor(name, shape, dt))

        def sem(name):
            return ctx.enter_context(nc.semaphore(name))

        x = sb("x", [P, KT, SEQ])
        h_hi = sb("h_hi", [P, KT, SEQ], F32R)
        h_lo = sb("h_lo", [P, KT, SEQ], F32R)
        stage = sb("stage", [P, RING, 1024])
        w_hi = sb("w_hi", [P, RING, 1024], F32R)
        w_lo = sb("w_lo", [P, RING, 1024], F32R)
        mod_stage = sb("mod_stage", [P, MOD_RING, D])
        mod_acc = sb("mod_acc", [P, D])
        tmp_a = sb("tmp_a", [P, 2, SEQ])
        tmp_b = sb("tmp_b", [P, 2, SEQ])
        rope_c = sb("rope_c", [P, SEQ])
        rope_s = sb("rope_s", [P, SEQ])
        ident = sb("ident", [P, P])
        ones = sb("ones", [P, P])
        cols = sb("cols", [P, 4])
        vcols = sb("vcols", [P, 88])
        modb = sb("modb", [P, DEPTH * N_MOD * KT])
        modc = sb("modc", [P, N_MOD, KT])
        c_silu = sb("c_silu", [P, KT])
        a_col = sb("a_col", [P, KT])
        gate = sb("gate", [P, 3, KT])
        half_bias = sb("half_bias", [P, ST])
        ms = sb("ms", [P, 4])
        rstd = sb("rstd", [P, 4])
        mhalf = sb("mhalf", [P, 4])
        NQ = 4 * GI
        s5_raw = sb("s5_raw", [G, 2, NS])
        s5_ldt = sb("s5_ldt", [P, NQ])
        s5_a = sb("s5_a", [P, 2, NQ])
        s5_t = sb("s5_t", [P, 14, NQ])
        pw = sb("pw", [P, 2, L + 1, NQ])
        en = sb("en", [P, 2, 6, NQ])
        fz = sb("fz", [P, 2, NQ])
        mag_l = sb("mag_l", [P, NQ])

        EARLY = ExitStack()
        x_in = sb("x_in", [P, QB, D], at=EARLY)
        vraw = sb("vraw", [P, 3, P], at=EARLY)
        pos_i = sb("pos_i", [P, SEQ], I32, at=EARLY)
        EARLY.close()
        FFN = ExitStack()
        g_hi = sb("g_hi", [P, FT, SEQ], F32R, at=FFN)
        g_lo = sb("g_lo", [P, FT, SEQ], F32R, at=FFN)
        FFN.close()
        MIX = ExitStack()
        q_t = sb("q_t", [P, AT, SEQ], at=MIX)
        k_t = sb("k_t", [P, SEQ], at=MIX)
        qi_t = sb("qi_t", [P, 2, SEQ], at=MIX)
        ki_t = sb("ki_t", [P, SEQ], at=MIX)
        z_t = sb("z_t", [P, 2, SEQ], at=MIX)
        u_t = sb("u_t", [P, ST, L, J], at=MIX)
        v_n = sb("v_n", [P, QB, HD], at=MIX)
        wi_n = sb("wi_n", [P, QB, IDX_HEADS], at=MIX)
        score_all = sb("score", [P, QB * (QB + 1) // 2 * P], at=MIX)
        score = [score_all[:, b * (b + 1) // 2 * P:(b + 1) * (b + 2) // 2 * P] for b in range(QB)]
        top8 = sb("top8", [P, 8], at=MIX)
        nmax = sb("nmax", [P, 2], at=MIX)
        rsum = sb("rsum", [P, HEADS], at=MIX)
        rinv = sb("rinv", [P, HEADS], at=MIX)
        att_ss = sb("att_ss", [P, 3], at=MIX)
        pt = sb("pt", [P, 2, SEQ], at=MIX)
        att = sb("att", [P, HEADS, HD], at=MIX)
        d_raw = sb("d_raw", [GC, G], at=MIX)
        ct = sb("ct", [P, 3, 4, GI * GC], at=MIX)
        bb = sb("bb", [P, 2, 4, GI * GC], at=MIX)
        pr = sb("pr", [P, 2, L, NQ], at=MIX)
        ca = sb("ca", [P, 2, 2, GI, L + 1, GC], at=MIX)
        ab = sb("ab", [P, 2, GI, L, GC], at=MIX)
        rot = sb("rot", [P, 2, 2, GI, J], at=MIX)
        dec = sb("dec", [P, 2, GI, J], at=MIX)
        pool_t = sb("pool_t", [P, GI * (L + 1) * GC], at=MIX)
        wst = sb("wst", [P, 2, GI, P], at=MIX)
        toep = sb("toep", [P, 2 * GI, P], at=MIX)
        kk_y = sb("kk_y", [NS, 2 * GI * P], at=MIX)
        un = sb("un", [J, 2 * GI, L, GC], at=MIX)
        hs = sb("hs", [P, 2, GI, J + 1], at=MIX)
        dtmp = sb("dtmp", [GC, 2 * GI, GC], at=MIX)
        with ExitStack() as first_half:
            swaps = sb("swaps", [P, 5, P], at=first_half)
            c_raw = sb("c_raw", [GI * GC, 2, 4, P], at=first_half)
            b_raw = sb("b_raw", [P, 2, 4, GI * GC], at=first_half)
        u8 = sb("u8", [P, 2 * GI, J], at=MIX)
        xr = sb("xr", [P, 2, GI, J], at=MIX)
        gr = sb("gr", [P, 2, GI, J], at=MIX)
        s5_m = sb("s5_m", [P, 2, GI, J], at=MIX)
        MIX.close()
        LATE = ExitStack()
        o_t = sb("o_t", [P, 2, SEQ], at=LATE)
        o_n = sb("o_n", [P, 2, QB, P], at=LATE)
        LATE.close()

        ps = ctx.enter_context(nc.psum_tensor("ps", [P, 8, 512], F32))

        in_x, in_pos, in_vec, in_const, in_c = (sem(n) for n in (
            "in_x", "in_pos", "in_vec", "in_const", "in_c"))
        s5_in = Signal(sem("s5_in"), 16 * 4)
        mix_in = Signal(sem("mix_in"), 16 * 26)
        w_loaded = [sem(f"w_loaded{i}") for i in range(RING)]
        w_split_hi = Signal(sem("w_split_hi"), LAYER_CHUNKS)
        w_split_lo = Signal(sem("w_split_lo"), LAYER_CHUNKS, RING)
        w_used = Signal(sem("w_used"), LAYER_CHUNKS, RING)
        m_loaded = [sem(f"m_loaded{i}") for i in range(MOD_RING)]
        MODS = N_MOD * KT
        m_used = Signal(sem("m_used"), MODS, MOD_RING + 2 * KT)
        acc_ready = Signal(sem("acc_ready"), N_MOD, 2)
        mod_psum = Signal(sem("mod_psum"), N_MOD, 2)
        mod_done = Signal(sem("mod_done"), N_MOD, 2)
        prologue = sem("prologue")
        prologue_d = sem("prologue_d")
        prologue_a = sem("prologue_a")
        credits = sem("credits")
        ms_ready = Signal(sem("ms_ready"), 4)
        rstd_ready = Signal(sem("rstd_ready"), 4)
        diag_ready = Signal(sem("diag_ready"), 4)
        bcast = Signal(sem("bcast"), 4)
        a_ready = Signal(sem("a_ready"), 3)
        ht_ready = Signal(sem("ht_ready"), 3 * KT)
        h_hi_done = Signal(sem("h_hi_done"), 3 * KT)
        h_done = Signal(sem("h_done"), 3 * KT)
        silu_done = Signal(sem("silu_done"), 2 * FT)
        g_full = Signal(sem("g_full"), 2 * FT, 2)
        g_hi_done = Signal(sem("g_hi_done"), 2 * FT)
        g_done = Signal(sem("g_done"), 2 * FT, 2)
        x_new = Signal(sem("x_new"), 3 * KT, KT + 2)
        sq_done = Signal(sem("sq_done"), 3 * KT, KT)
        ssq = Signal(sem("ssq"), 3 * KT, KT + 2)
        z_copy = Signal(sem("z_copy"), 12)
        swap_mm = Signal(sem("swap_mm"), 8)
        rope_done = Signal(sem("rope_done"), 8)
        v_tr = Signal(sem("v_tr"), 1)
        v_done = Signal(sem("v_done"), 2)
        idx_mm = Signal(sem("idx_mm"), 12)
        idx_relu = Signal(sem("idx_relu"), 12)
        idx_acc = Signal(sem("idx_acc"), 12)
        mask_done = Signal(sem("mask_done"), QB)
        NA = QB * HEADS
        logit = Signal(sem("logit"), NA)
        masked = Signal(sem("masked"), NA)
        p_exp = Signal(sem("p_exp"), NA)
        pt_mm = Signal(sem("pt_mm"), NA)
        pt_copy = Signal(sem("pt_copy"), NA)
        pv = Signal(sem("pv"), NA)
        att_n = Signal(sem("att_n"), QB)
        att_sq = Signal(sem("att_sq"), QB)
        att_ms = Signal(sem("att_ms"), QB)
        att_rs = Signal(sem("att_rs"), QB)
        att_sc = Signal(sem("att_sc"), QB)
        att_tr = Signal(sem("att_tr"), QB)
        att_f = Signal(sem("att_f"), QB)
        att_hi = Signal(sem("att_hi"), QB)
        att_done = Signal(sem("att_done"), QB)
        s5_act = Signal(sem("s5_act"), 5)
        s5_sel = Signal(sem("s5_sel"), 1)
        s5_vec = Signal(sem("s5_vec"), 2)
        ct_mm = Signal(sem("ct_mm"), 1)
        ct_done = Signal(sem("ct_done"), 3)
        bb_done = Signal(sem("bb_done"), 1)
        toep0 = Signal(sem("toep0"), 1)
        prep = Signal(sem("prep"), 4)
        kk_mm = Signal(sem("kk_mm"), 4)
        kk_copy = Signal(sem("kk_copy"), 4 * 2)
        kk_d = Signal(sem("kk_d"), 4)
        toep_in = Signal(sem("toep_in"), 4 * 16 * L)
        w_tr = Signal(sem("w_tr"), 4)
        w_copy = Signal(sem("w_copy"), 4 * 2)
        un_tr = Signal(sem("un_tr"), 4)
        un_copy = Signal(sem("un_copy"), 4 * 2)
        u8_tr = Signal(sem("u8_tr"), 4)
        u8_copy = Signal(sem("u8_copy"), 4)
        st_mm = Signal(sem("st_mm"), 4)
        hs_done = Signal(sem("hs_done"), 4)
        y_mm = Signal(sem("y_mm"), 4)
        y_copy = Signal(sem("y_copy"), 4 * 2)
        y_tr = Signal(sem("y_tr"), 4)
        y_act = Signal(sem("y_act"), 4 * 2)
        y_done = Signal(sem("y_done"), 4)
        glu_act = Signal(sem("glu_act"), ST)
        ssm_y = Signal(sem("ssm_y"), ST)
        ssm_sq = Signal(sem("ssm_sq"), ST)
        ssm_ss = Signal(sem("ssm_ss"), ST)
        ssm_f = Signal(sem("ssm_f"), ST)
        ssm_hi = Signal(sem("ssm_hi"), ST)
        mix_done = Signal(sem("mix_done"), ST)
        out_f = sem("out_f")
        out_tr = sem("out_tr")
        out_copy = sem("out_copy")
        out_dma = [sem(f"out_dma{i}") for i in range(2)]
        dve_step = sem("dve_step")
        pool_step = sem("pool_step")
        settled = sem("settled")

        w1 = [a["ffn1_w1"], a["ffn2_w1"]]
        w3 = [a["ffn1_w3"], a["ffn2_w3"]]
        w2 = [a["ffn1_w2"], a["ffn2_w2"]]

        def tiles(w, layer, k0, k, col, width=P):
            v = w.rearrange("l (k p) n -> l p k n", p=P)
            return v[ds(layer, 1), :, k0:k0 + k, ds(col, width)].rearrange("a p k n -> (a p) k n")

        def wait(eng, s, layer, k):
            eng.wait_ge(s.sem, s.after(layer, k))

        def settle(eng):
            eng.sem_inc(settled, 1)

        def used(eng, layer, c, shift=0):
            eng.wait_ge(w_used.sem, w_used.after(layer, c) + shift)

        def projected(eng, layer, e):
            n = e % KT
            used(eng, layer, MIX_BASE + 16 + n if e // KT == 1 else FFN_BASE[e // (2 * KT)] + 2 * FT + 3 * n + 2)

        def loads(c):
            return 2 if c % LAYER_CHUNKS in (MIX_BASE + 2, MIX_BASE + 3) else 1

        def slot_loaded(layer, c, turns):
            total = sum(loads(e) for e in range(c % RING, LAYER_CHUNKS, RING))
            upto = sum(loads(e) for e in range(c % RING, c + 1, RING))
            return 16 * total * layer + 16 * upto + 16 // RING * turns

        def down_chunk(j):
            return sum(DOWN_K[:j]), DOWN_K[j]

        def chunk_size(c):
            c %= LAYER_CHUNKS
            for b in FFN_BASE:
                if b + 2 * FT <= c < b + FFN_CHUNKS:
                    return DOWN_K[(c - b - 2 * FT) % 3] * P
            if MIX_BASE + 8 + ST <= c < MIX_BASE + 8 + 2 * ST:
                return ST * P
            return KT * P

        block = ctx.enter_context(nc.Block())

        @block.sync
        def _(sp):
            def load_w(layer, c, src, extra=0, shift=0):
                n = chunk_size(c)
                sp.wait_ge(w_split_lo.sem, w_split_lo.after(layer, c - RING) + shift)
                settle(sp)
                dst = stage[:, c % RING, 0:n]
                src = src if isinstance(src, tuple) else (src,)
                dst = dst.rearrange("p (k t n) -> p k t n", k=src[0].shape[1], t=len(src))
                for t, v in enumerate(src):
                    sp.dma_start(dst[:, :, t, :], v).then_inc(w_loaded[c % RING], 16)

            def load_mod(layer, q, src_layer, part, shift=0):
                sp.wait_ge(m_used.sem, m_used.after(layer, q - MOD_RING) + shift)
                src = a["mod_w"].rearrange("l k n -> (l k) n")[
                    ds(src_layer * D + (q % KT) * P, P), ds(part * D, D)]
                sp.dma_start(mod_stage[:, q % MOD_RING, :], src).then_inc(m_loaded[q % MOD_RING], 16)

            def load_up(layer, ffn, f, c, shift=0):
                load_w(layer, c, tiles(w1[ffn], layer, 0, KT, f * P), shift=shift)
                load_w(layer, c + 1, tiles(w3[ffn], layer, 0, KT, f * P), shift=shift)

            def mix_src(layer, m):
                w_in = a["w_in"]
                if m < 2:
                    return tiles(w_in, layer, 0, KT, COL_QI + m * P)
                if m in (2, 3):
                    col = COL_K if m == 2 else COL_K + HD
                    return tuple(tiles(w_in, layer, 0, KT, col + t * (COL_KI - COL_K), HD) for t in range(2))
                if m < 8:
                    return tiles(w_in, layer, 0, KT, (m - 4) * P)
                if m < 12:
                    return tiles(w_in, layer, 0, KT, COL_U + (m - 8) * P)
                if m < 16:
                    return tiles(a["glu_w"], layer, 0, ST, (m - 12) * P)
                return tiles(a["w_out"], layer, 0, KT, (m - 16) * P)

            def following(layer, ffn, m):
                if ffn == 0:
                    return mix_src(layer, m)
                return tiles((w1[0], w3[0])[m], (layer + 1) % DEPTH, 0, KT, 0)

            sp.dma_start(vraw[80:88, 0, :], a["c"].rearrange("o (k p) -> (o k) p", p=P)).then_inc(in_c, 16)
            sp.dma_start(vraw[0:48, 0, :], a["norm_g"].rearrange("l t (k p) -> (l t k) p", p=P)).then_inc(in_c, 16)
            sp.dma_start(vraw[48:56, 0, :], a["final_g"].rearrange("(k p) -> k p", p=P)).then_inc(in_c, 16)
            sp.dma_start(vraw[56:64, 0, :], a["attn_gain"].rearrange("l (k p) -> (l k) p", p=P)).then_inc(in_c, 16)
            sp.dma_start(vraw[64:72, 0, :], a["ssm_gain"].rearrange("l (k p) -> (l k) p", p=P)).then_inc(in_c, 16)
            sp.dma_start(vraw[72:80, 0, :], a["glu_b"].rearrange("l (k p) -> (l k) p", p=P)).then_inc(in_c, 16)
            sp.dma_start(ident[:], a["consts"][:, C_ID:C_ID + P]).then_inc(in_const, 16)
            sp.dma_start(cols[:], a["consts"][:, C_COLS:C_COLS + 4]).then_inc(in_const, 16)
            for l in range(DEPTH):
                sp.dma_start(vraw[0:72, 1 + l, :], a["mod_b"][l].rearrange("(k p) -> k p", p=P)).then_inc(in_vec, 16)
            sp.dma_start(pos_i[:], a["positions"].partition_broadcast(P).rearrange("p o t -> p (o t)")).then_inc(in_pos, 16)
            for q in range(2 * KT):
                if q == 2:
                    sp.dma_start(x_in[:], a["x"].rearrange("o (b p) d -> p (o b) d", p=P)).then_inc(in_x, 16)
                load_mod(0, q - 2 * KT, 0, q // KT)
            load_w(0, 0, tiles(w1[0], 0, 0, KT, 0))
            load_w(0, 1, tiles(w3[0], 0, 0, KT, 0))

            with sp.Fori(0, DEPTH) as l:
                for ffn in range(2):
                    c0 = FFN_BASE[ffn]
                    if ffn == 0:
                        for i, name in enumerate(("ssm_a_re", "ssm_a_im")):
                            sp.dma_start(s5_raw[:, i, :], a[name][ds(l, 1)].rearrange("o g p -> (o g) p")).then_inc(s5_in.sem, 16)
                        for g2 in range(2):
                            v = a["ssm_log_dt"][ds(l, 1)].rearrange("o (m t i) -> t o m i", t=2, i=GI)[g2]
                            sp.dma_start(s5_ldt[g2 * NS:(g2 + 1) * NS, :].rearrange("p (m i) -> p m i", i=GI),
                                         v.rearrange("o m i -> (o m) i").partition_broadcast(NS)).then_inc(s5_in.sem, 16)
                    with sp.Fori(0, A_TURNS) as i:
                        for u in range(A_UNROLL):
                            load_up(l, ffn, A_UNROLL * i + (u + 1), c0 + 2 * (u + 1), shift=2 * A_UNROLL * i)
                            if ffn == 0:
                                for q in (2 * u, 2 * u + 1):
                                    load_mod(l, q, l, i + 2, shift=KT * i)
                    last = A_TURNS * A_UNROLL
                    q0 = A_TURNS * KT if ffn == 0 else (A_TURNS + 1) * KT
                    for f in (last, last + 1):
                        c = c0 + 2 * (f + 1)
                        if f == last:
                            load_up(l, ffn, f + 1, c)
                        else:
                            for j in range(2):
                                load_w(l, c + j, tiles(w2[ffn], l, *down_chunk(j), 0))
                        for q in range(4 * (f - last), 4 * (f - last) + 4):
                            load_mod(l, q0 + q, l, 7 + ffn)
                    b0 = c0 + 2 * FT
                    for n in range(KT):
                        for e in range(3 * n + AHEAD, 3 * n + AHEAD + 3):
                            if e < 3 * KT:
                                load_w(l, b0 + e, tiles(w2[ffn], l, *down_chunk(e % 3), (e // 3) * P))
                            else:
                                load_w(l, b0 + e, following(l, ffn, e - 3 * KT))
                        if ffn == 1:
                            for q in (2 * n, 2 * n + 1):
                                load_mod(l, q0 + KT + q, (l + 1) % DEPTH, q // KT)
                    if ffn == 0:
                        projected(sp, l, KT - 1)
                        for i in range(5):
                            sp.dma_start(swaps[:, i, :], a["consts"][:, (i + 1) * P:(i + 2) * P]).then_inc(mix_in.sem, 16)
                        for i, name in enumerate(("ssm_c_re", "ssm_c_im")):
                            v = a[name][ds(l, 1)].rearrange("o (m t i) c p -> o (i c) m t p", t=2, i=GI)
                            v = v.rearrange("o q m t p -> (o q) m t p")
                            for g2 in range(2):
                                sp.dma_start(c_raw[:, i, :, g2 * NS:(g2 + 1) * NS], v[:, :, g2, :]).then_inc(mix_in.sem, 16)
                        for i, name in enumerate(("ssm_b_re", "ssm_b_im")):
                            for g2 in range(2):
                                v = a[name][ds(l, 1)].rearrange("o (m t i) p c -> m t o p i c", t=2, i=GI)
                                for m in range(4):
                                    sp.dma_start(b_raw[g2 * NS:(g2 + 1) * NS, i, m, :].rearrange("p (i c) -> p i c", i=GI),
                                                 v[m, g2].rearrange("o p i c -> (o p) i c")).then_inc(mix_in.sem, 16)
                        sp.dma_start(d_raw[:], a["ssm_d"][ds(l, 1)].rearrange("o g c -> c (o g)"), allow_slow_non_contiguous=True).then_inc(mix_in.sem, 16)
                        for m in range(AHEAD, MIX_CHUNKS + AHEAD):
                            if m < MIX_CHUNKS:
                                load_w(l, MIX_BASE + m, mix_src(l, m))
                            else:
                                w = (w1[1], w3[1])[m - MIX_CHUNKS]
                                load_w(l, MIX_BASE + m, tiles(w, l, 0, KT, 0))

        @block.scalar
        def _(act):
            def split_hi(layer, c, shift=0):
                n, turns = chunk_size(c), shift
                act.wait_ge(w_loaded[c % RING], slot_loaded(layer, c, turns))
                act.wait_ge(w_used.sem, w_used.after(layer, c - RING) + turns)
                nc.scalar.activation(w_hi[:, c % RING, 0:n], stage[:, c % RING, 0:n], ACT.Copy).then_inc(w_split_hi.sem, 1)

            def squares(layer, k):
                wait(act, x_new, layer, k)
                wait(act, ssq, layer, k - 2)
                nc.scalar.activation(tmp_b[:, k % 2, :], x[:, k % KT, :], ACT.Square).then_inc(sq_done.sem, 1)

            def norm_hi(layer, k3, shift_part):
                wait(act, a_ready, layer, k3)
                for k in range(KT):
                    e = k3 * KT + k
                    wait(act, ht_ready, layer, e)
                    nc.scalar.activation(h_hi[:, k, :], tmp_a[:, k % 2, :], ACT.Identity, scale=a_col[:, k:k + 1],
                                         bias=modc[:, shift_part, k:k + 1]).then_inc(h_hi_done.sem, 1)

            act.wait_ge(credits, 6)
            nc.scalar.activation(c_silu[:], vcols[:, 80:88], ACT.Silu).then_inc(prologue_a, 1)
            act.wait_ge(prologue_d, 1)
            nc.scalar.activation(rope_s[:], tmp_a[:, 0, :], ACT.Sin).then_inc(prologue_a, 1)
            nc.scalar.activation(rope_c[:], tmp_a[:, 1, :], ACT.Sin).then_inc(prologue_a, 1)
            for k in range(KT):
                squares(0, k - KT)
            for c in range(AHEAD):
                split_hi(0, c)

            def ffn_act(l, ffn):
                c0, f0 = FFN_BASE[ffn], ffn * FT

                def tile(f, parity, shift):
                    used(act, l, c0 + 2 * f + 1, 2 * shift)
                    nc.scalar.activation(tmp_a[:, parity, :], ps[:, 2 * parity, :], ACT.Silu).then_inc(silu_done.sem, 1)
                    act.wait_ge(g_full.sem, g_full.after(l, f0 + f) + shift)
                    nc.scalar.activation(g_hi[:, ds(f + shift, 1), :].rearrange("p a n -> p (a n)") if not isinstance(shift, int) else g_hi[:, f, :],
                                         tmp_b[:, parity, :], ACT.Copy).then_inc(g_hi_done.sem, 1)

                with act.Fori(0, A_TURNS) as i:
                    for u in range(A_UNROLL):
                        for j in range(2):
                            split_hi(l, c0 + 2 * (u + 1) + j, shift=2 * A_UNROLL * i)
                        tile(u, u % 2, A_UNROLL * i)
                for f in (FT - 2, FT - 1):
                    for j in range(2):
                        split_hi(l, c0 + 2 * (f + 1) + j)
                    tile(f, f % 2, 0)
                for n in range(KT):
                    for e in range(3 * n + AHEAD, 3 * n + AHEAD + 3):
                        split_hi(l, c0 + 2 * FT + e)
                    squares(l, 2 * KT * ffn + n)

            def s5_constants(l):
                wait(act, s5_sel, l, 0)
                nc.scalar.activation(s5_a[:].rearrange("p t q -> p (t q)"), ps[:, 6, 16:16 + 2 * NQ], ACT.Copy).then_inc(s5_act.sem, 1)
                act.wait_ge(s5_in.sem, 64 * l + 64)
                nc.scalar.activation(s5_t[:, 0, :], s5_ldt[:], ACT.Exp).then_inc(s5_act.sem, 1)
                wait(act, s5_vec, l, 0)
                nc.scalar.activation(s5_t[:, 3, :], s5_t[:, 1, :], ACT.Exp).then_inc(s5_act.sem, 1)
                nc.scalar.activation(mag_l[:], s5_t[:, 1, :], ACT.Exp, scale=float(L)).then_inc(s5_act.sem, 1)
                wait(act, s5_vec, l, 1)
                nc.scalar.activation(s5_t[:, 6:8, :].rearrange("p t q -> p (t q)"),
                                     s5_t[:, 4:6, :].rearrange("p t q -> p (t q)"), ACT.Sin).then_inc(s5_act.sem, 1)

            def mixer_act(l):
                m0 = MIX_BASE

                def z_tile(t):
                    used(act, l, m0 + t)
                    if t < 8:
                        if t in (2, 3):
                            wait(act, rope_done, l, t - 2)
                        elif t == 4:
                            wait(act, rope_done, l, 3)
                        elif t == 5:
                            wait(act, v_tr, l, 0)
                        elif t > 5:
                            wait(act, rope_done, l, t - 2)
                        nc.scalar.activation(z_t[:, t % 2, :], ps[:, t % 2, :], ACT.Copy).then_inc(z_copy.sem, 1)
                    else:
                        nc.scalar.activation(u_t[:, t - 8, :, :], ps[:, t % 2, :].rearrange("p (j s) -> p s j", s=L),
                                             ACT.Copy).then_inc(z_copy.sem, 1)

                def index_relu(n):
                    b = n // IDX_HEADS + 1
                    wait(act, idx_mm, l, n)
                    if n >= 2:
                        wait(act, idx_acc, l, n - 2)
                    w = (b + 1) * P
                    nc.scalar.activation(tmp_a[:, n % 2, 0:w], ps[:, 4 + n % 2, 0:w], ACT.Relu).then_inc(idx_relu.sem, 1)

                def v_copy():
                    wait(act, v_tr, l, 0)
                    v = ps[:, 4, :].rearrange("p (b n) -> p b n", b=QB)
                    nc.scalar.activation(v_n[:], v[:, :, 0:HD], ACT.Copy).then_inc(v_done.sem, 1)
                    nc.scalar.activation(wi_n[:], v[:, :, HD:HD + IDX_HEADS], ACT.Copy, scale=IDX_SCALE).then_inc(v_done.sem, 1)

                def ct_copy():
                    wait(act, ct_mm, l, 0)
                    v = ps[:, 7, :].rearrange("p (t n) -> p t n", t=2)
                    for i, (src, scale) in enumerate(((0, 1.0), (1, 1.0), (0, -1.0))):
                        nc.scalar.activation(ct[:, i, :, :].rearrange("p m q -> p (m q)"), v[:, src, :], ACT.Copy,
                                             scale=scale).then_inc(ct_done.sem, 1)

                def p_head(e):
                    b, h = e // HEADS, e % HEADS
                    w = (b + 1) * P
                    wait(act, masked, l, e)
                    if e >= 2:
                        wait(act, pt_mm, l, e - 2)
                    if h == 0 and b > 0:
                        wait(act, att_n, l, b - 1)
                    nc.scalar.activation(tmp_b[:, e % 2, 0:w], tmp_a[:, e % 2, 0:w], ACT.Exp, scale=-1.0,
                                         bias=nmax[:, e % 2:e % 2 + 1], accum_out=rsum[:, h:h + 1]).then_inc(p_exp.sem, 1)
                    wait(act, pt_mm, l, e)
                    if e >= 2:
                        wait(act, pv, l, e - 2)
                    nc.scalar.activation(pt[:, e % 2, 0:w], ps[:, 2, 0:w], ACT.Copy).then_inc(pt_copy.sem, 1)

                def att_act(b):
                    wait(act, att_n, l, b)
                    nc.scalar.activation(tmp_b[:, 0, :], att[:].rearrange("p h d -> p (h d)"), ACT.Square,
                                         accum_out=att_ss[:, 0:1]).then_inc(att_sq.sem, 1)
                    wait(act, att_f, l, b)
                    nc.scalar.activation(h_hi[:, 0:AT, b * P:(b + 1) * P], tmp_b[:, 1, :].rearrange("p (m t) -> p m t", m=AT),
                                         ACT.Copy).then_inc(att_hi.sem, 1)

                def half(i):
                    return slice(i * 512, (i + 1) * 512)

                def s5_kk(m):
                    wait(act, kk_mm, l, m)
                    for i in range(2):
                        nc.scalar.activation(kk_y[0:GC, half(i)], ps[0:GC, 4 + i, :], ACT.Copy).then_inc(kk_copy.sem, 1)
                    wait(act, kk_d, l, m)
                    wait(act, toep0, l, 0)
                    kk = kk_y[0:GC, :].rearrange("c (g n) -> c g n", g=2 * GI)
                    for s in range(L):
                        act.dma_start(toep[s * GC:(s + 1) * GC, :, s * GC:P], kk[:, :, 0:P - s * GC]).then_inc(toep_in.sem, 16)

                def s5_w(m):
                    wait(act, w_tr, l, m)
                    for i in range(2):
                        nc.scalar.activation(wst[:, i, :, :].rearrange("p i n -> p (i n)"), ps[:, 4 + i, :], ACT.Copy).then_inc(w_copy.sem, 1)

                def s5_un(m):
                    wait(act, un_tr, l, m)
                    for i in range(2):
                        nc.scalar.activation(un[:, :, 4 * i:4 * i + 4, :].rearrange("j g s c -> j s g c"),
                                             ps[0:J, 4 + i, :].rearrange("j (s g c) -> j s g c", s=4, c=GC),
                                             ACT.Copy).then_inc(un_copy.sem, 1)

                def s5_u8(m):
                    wait(act, u8_tr, l, m)
                    nc.scalar.activation(u8[:].rearrange("p g j -> p (g j)"), ps[:, 4, :], ACT.Copy).then_inc(u8_copy.sem, 1)

                def s5_y(m):
                    wait(act, y_mm, l, m)
                    act.wait_ge(toep_in.sem, toep_in.per * l + 16 * L * (m + 1))
                    for i in range(2):
                        nc.scalar.activation(kk_y[:].rearrange("j (t g c) -> j g t c", t=L, c=GC)[:, 4 * i:4 * i + 4],
                                             ps[0:J, 4 + i, :].rearrange("j (g t c) -> j g t c", g=4, c=GC),
                                             ACT.Copy).then_inc(y_copy.sem, 1)
                    wait(act, y_tr, l, m)
                    if m:
                        wait(act, y_done, l, m - 1)
                    nc.scalar.activation(z_t[:, 0, :].rearrange("p (j t) -> p j t", t=L),
                                         ps[:, 6, :].rearrange("p (t j) -> p j t", t=L), ACT.Gelu_apprx_tanh).then_inc(y_act.sem, 1)
                    wait(act, y_act, l, 2 * m)
                    nc.scalar.activation(h_hi[:, AT + m, :], z_t[:, 0, :], ACT.Copy).then_inc(y_act.sem, 1)

                norm_hi(l, 1, 3)
                for t in range(12):
                    split_hi(l, m0 + t + AHEAD)
                    z_tile(t)
                    if t == 2:
                        ct_copy()
                    if t == 4:
                        v_copy()
                    if t in (6, 7, 8):
                        for n in range(IDX_HEADS):
                            index_relu((t - 6) * IDX_HEADS + n)
                wait(act, h_done, l, 2 * KT - 1)
                for b in range(QB):
                    steps = {0: s5_kk, 1: s5_w, 2: s5_un, 3: s5_u8}
                    for h in range(HEADS):
                        p_head(b * HEADS + h)
                        if h in steps:
                            steps[h](b)
                    att_act(b)
                    s5_y(b)
                for n in range(ST):
                    split_hi(l, m0 + 12 + n + AHEAD)
                for n in range(ST):
                    used(act, l, m0 + 12 + n)
                    if n >= 2:
                        wait(act, ssm_y, l, n - 2)
                    if n == 0:
                        wait(act, y_done, l, 3)
                    nc.scalar.activation(tmp_a[:, n % 2, :], ps[:, n, :], ACT.Tanh, scale=0.5,
                                         bias=half_bias[:, n:n + 1]).then_inc(glu_act.sem, 1)
                    wait(act, ssm_y, l, n)
                    if n >= 2:
                        wait(act, ssm_ss, l, n - 2)
                    nc.scalar.activation(tmp_b[:, n % 2, :], q_t[:, n, :], ACT.Square).then_inc(ssm_sq.sem, 1)
                for n in range(ST):
                    wait(act, ssm_f, l, n)
                    nc.scalar.activation(h_hi[:, AT + n, :], tmp_a[:, n % 2, :], ACT.Copy).then_inc(ssm_hi.sem, 1)
                for n in range(KT):
                    split_hi(l, m0 + 16 + n + AHEAD)
                    squares(l, KT + n)

            with act.Fori(0, DEPTH) as l:
                norm_hi(l, 0, 0)
                s5_constants(l)
                ffn_act(l, 0)
                mixer_act(l)
                norm_hi(l, 2, 6)
                ffn_act(l, 1)

            for n in range(KT):
                act.wait_ge(out_tr, n + 1)
                if n >= 2:
                    act.wait_ge(out_dma[n % 2], 16 * (n // 2))
                nc.scalar.activation(o_n[:, n % 2, :, :].rearrange("p b f -> p (b f)"), ps[:, 4 + n % 2, :], ACT.Copy).then_inc(out_copy, 1)
                act.wait_ge(out_copy, n + 1)
                act.dma_start(a["out"].rearrange("o (b p) d -> p (o b) d", p=P)[:, :, n * P:(n + 1) * P],
                              o_n[:, n % 2, :, :]).then_inc(out_dma[n % 2], 16)
            for i in range(2):
                act.wait_ge(out_dma[i], 16 * KT // 2)

        @block.vector
        def _(dve):
            V = nc.vector

            def split_lo(layer, c, shift=0):
                n = chunk_size(c)
                dve.wait_ge(w_split_hi.sem, w_split_hi.after(layer, c) + shift)
                V.tensor_tensor(w_lo[:, c % RING, 0:n], stage[:, c % RING, 0:n],
                                w_hi[:, c % RING, 0:n].bitcast(F32), ALU.subtract).then_inc(w_split_lo.sem, 1)

            def mod_chunk(layer, q, shift=0, turn=0):
                s, turns = q % MOD_RING, shift
                per = MODS // MOD_RING
                dve.wait_ge(m_loaded[s], 16 * (layer * per + (q + 2 * KT) // MOD_RING + 1) + 16 // MOD_RING * turns)
                dve.wait_ge(m_used.sem, m_used.after(layer, q - 1) + turns)
                if q % KT == 0 and q > -2 * KT:
                    dve.wait_ge(mod_psum.sem, mod_psum.after(layer, q // KT - 1) + turn)
                k = q % KT
                if k == 0:
                    i = V.tensor_scalar(mod_acc[:], mod_stage[:, s, :], c_silu[:, k:k + 1], None, ALU.mult)
                else:
                    i = V.scalar_tensor_tensor(out=mod_acc[:], in0=mod_stage[:, s, :], scalar=c_silu[:, k:k + 1],
                                               in1=mod_acc[:], op0=ALU.mult, op1=ALU.add)
                i.then_inc(m_used.sem, 1)

            def mod_out(layer, j, part, bias_layer, turn=0):
                dve.wait_ge(mod_psum.sem, mod_psum.after(layer, j) + turn)
                V.tensor_tensor(modc[:, ds(part, 1), :].rearrange("p a k -> p (a k)") if not isinstance(part, int) else modc[:, part, :],
                                ps[:, 7, 0:KT], modb[:, ds(bias_layer * (N_MOD * KT) + part * KT, KT)],
                                ALU.add).then_inc(mod_done.sem, 1)

            def rms(layer, idx, width, step):
                V.tensor_scalar(ms[:], ps[:, 6, 0:QB], 1.0 / width, EPS, ALU.mult, ALU.add).then_inc(ms_ready.sem, 1)
                wait(dve, rstd_ready, layer, idx)
                V.tensor_tensor(tmp_b[:, 0, :].rearrange("p (b t) -> p b t", b=QB),
                                ident[:].unsqueeze(1).broadcast_to((P, QB, P)),
                                rstd[:].unsqueeze(2).broadcast_to((P, QB, P)), ALU.mult).then_inc(diag_ready.sem, 1)

            def norm(layer, k3, idx, scale_part, shift_part, gate_part, gate_scale, step):
                wait(dve, ssq, layer, KT * k3 - 1)
                rms(layer, idx, D, step)
                wait(dve, mod_done, layer, scale_part - 2)
                V.scalar_tensor_tensor(out=a_col[:], in0=modc[:, scale_part, :], scalar=1.0,
                                       in1=vcols[:, ds(layer * (3 * KT) + k3 * KT, KT)],
                                       op0=ALU.add, op1=ALU.mult).then_inc(a_ready.sem, 1)
                wait(dve, bcast, layer, idx)

                def full_lo(k):
                    e = k3 * KT + k
                    step(V.tensor_scalar(tmp_b[:, k % 2, :], tmp_a[:, k % 2, :], a_col[:, k:k + 1],
                                         modc[:, shift_part, k:k + 1], ALU.mult, ALU.add))
                    wait(dve, h_hi_done, layer, e)
                    V.tensor_tensor(h_lo[:, k, :], tmp_b[:, k % 2, :], h_hi[:, k, :].bitcast(F32),
                                    ALU.subtract).then_inc(h_done.sem, 1)

                for k in range(KT + 1):
                    if k < KT:
                        e = k3 * KT + k
                        if k == 0:
                            wait(dve, a_ready, layer, k3)
                        if k >= 2:
                            wait(dve, h_done, layer, e - 2)
                        V.tensor_tensor(tmp_a[:, k % 2, :], x[:, k, :], ps[:, 7, :], ALU.mult).then_inc(ht_ready.sem, 1)
                    if k >= 1:
                        wait(dve, ht_ready, layer, k3 * KT + k - 1)
                        full_lo(k - 1)

            def gates(layer, k3, gate_part, gate_scale):
                wait(dve, mod_done, layer, gate_part - 2)
                return V.tensor_scalar(gate[:, k3, :], modc[:, gate_part, :], gate_scale, None, ALU.mult)

            def update(layer, k3, n):
                e = k3 * KT + n
                projected(dve, layer, e)
                V.scalar_tensor_tensor(out=x[:, n, :], in0=ps[:, 4 + n % 2, :], scalar=gate[:, k3, n:n + 1],
                                       in1=x[:, n, :], op0=ALU.mult, op1=ALU.add).then_inc(x_new.sem, 1)

            def reduce_angle(step, z, n, r):
                step(V.tensor_scalar(n, z, INV_2PI, ROUND, ALU.mult, ALU.add))
                step(V.tensor_scalar(n, n, ROUND, None, ALU.subtract))
                step(V.scalar_tensor_tensor(out=r, in0=n, scalar=-TWO_PI_A, in1=z, op0=ALU.mult, op1=ALU.add))
                step(V.scalar_tensor_tensor(out=r, in0=n, scalar=-TWO_PI_B, in1=r, op0=ALU.mult, op1=ALU.add))
                step(V.scalar_tensor_tensor(out=r, in0=n, scalar=-TWO_PI_C, in1=r, op0=ALU.mult, op1=ALU.add))
                step(V.tensor_scalar(r, r, float(np.float32(np.pi)) - 3e-7, -float(np.float32(np.pi)) + 3e-7, ALU.min, ALU.max))

            def cos_angle(step, r, c):
                step(V.tensor_scalar(c, r, -1.0, None, ALU.mult))
                step(V.tensor_tensor(c, c, r, ALU.max))
                step(V.tensor_scalar(c, c, -1.0, HALF_PI, ALU.mult, ALU.add))

            first = Chain(dve, credits, 0, 0)
            first(V.memset(ones[:], 1.0), V.memset(mhalf[:], -0.5))
            V.memset(ms[:, 0:1], 0.0).then_inc(w_split_lo.sem, RING)
            V.memset(ms[:, 1:2], 0.0).then_inc(w_used.sem, RING)
            V.memset(ms[:, 2:3], 0.0).then_inc(m_used.sem, MOD_RING)
            V.memset(ms[:, 3:4], 0.0).then_inc(g_full.sem, 2)
            V.memset(rstd[:, 3:4], 0.0).then_inc(g_done.sem, 2)
            V.memset(rstd[:, 0:1], 0.0).then_inc(x_new.sem, 2)
            V.memset(rstd[:, 1:2], 0.0).then_inc(ssq.sem, 2)
            first(V.memset(rstd[:, 2:3], 0.0))
            dve.wait_ge(prologue, 3)
            first(V.tensor_copy(vcols[:], ps[:, 4, 0:88]), V.tensor_copy(modb[:, 0:72], ps[:, 5, 0:72]),
                  V.tensor_copy(modb[:, 72:144], ps[:, 5, 128:200]))
            dve.wait_ge(in_pos, 16)
            dve.wait_ge(in_const, 32)
            ang, cnt = tmp_b[:, 0, :], tmp_b[:, 1, :]
            first(V.tensor_copy(ang, pos_i[:]))
            first(V.tensor_scalar(ang, ang, cols[:, 0:1], None, ALU.mult))
            reduce_angle(first, ang, cnt, tmp_a[:, 0, :])
            cos_angle(first, tmp_a[:, 0, :], tmp_a[:, 1, :])
            V.memset(s5_t[:, 0, 0:1], 0.0).then_inc(prologue_d, 1)
            dve.wait_ge(prologue_a, 3)
            first(V.tensor_scalar(rope_s[:], rope_s[:], cols[:, 1:2], None, ALU.mult),
                  V.tensor_scalar(rope_c[:], rope_c[:], cols[:, 2:3], cols[:, 3:4], ALU.mult, ALU.add))
            for q in range(2 * KT):
                mod_chunk(0, q - 2 * KT)
                if q % KT == KT - 1:
                    dve.wait_ge(m_used.sem, m_used.after(0, q - 2 * KT))
                    V.memset(s5_t[:, 1, q // KT:1 + q // KT], 0.0).then_inc(acc_ready.sem, 1)
                    mod_out(0, q // KT - 2, q // KT, 0)
            for n in range(KT):
                dve.wait_ge(prologue, 4 + n)
                V.tensor_copy(x[:, n, :], ps[:, 4 + n % 2, :]).then_inc(x_new.sem, 1)
            for c in range(AHEAD):
                split_lo(0, c)

            def acc_done(layer, q, slot, shift=0):
                dve.wait_ge(m_used.sem, m_used.after(layer, q) + shift)
                V.memset(s5_t[:, 13, slot:slot + 1], 0.0).then_inc(acc_ready.sem, 1)

            def ffn_dve(l, ffn):
                c0, f0 = FFN_BASE[ffn], ffn * FT
                q0 = A_TURNS * KT if ffn == 0 else (A_TURNS + 1) * KT

                def product(f, parity, shift):
                    dve.wait_ge(silu_done.sem, silu_done.after(l, f0 + f) + shift)
                    dve.wait_ge(g_done.sem, g_done.after(l, f0 + f - 2) + shift)
                    V.tensor_tensor(tmp_b[:, parity, :], tmp_a[:, parity, :], ps[:, 2 * parity + 1, :], ALU.mult).then_inc(g_full.sem, 1)

                def product_lo(f, parity, shift):
                    dve.wait_ge(g_hi_done.sem, g_hi_done.after(l, f0 + f) + shift)
                    static = isinstance(shift, int)
                    hi = g_hi[:, f, :] if static else g_hi[:, ds(f + shift, 1), :].rearrange("p a n -> p (a n)")
                    lo = g_lo[:, f, :] if static else g_lo[:, ds(f + shift, 1), :].rearrange("p a n -> p (a n)")
                    V.tensor_tensor(lo, tmp_b[:, parity, :], hi.bitcast(F32), ALU.subtract).then_inc(g_done.sem, 1)

                settle(dve)
                with dve.Fori(0, A_TURNS) as i:
                    for u in range(A_UNROLL):
                        for j in range(2):
                            split_lo(l, c0 + 2 * (u + 1) + j, shift=2 * A_UNROLL * i)
                        if ffn == 0:
                            mod_chunk(l, 2 * u, shift=KT * i, turn=i)
                        product(u, u % 2, A_UNROLL * i)
                        if ffn == 0:
                            mod_chunk(l, 2 * u + 1, shift=KT * i, turn=i)
                            if u == A_UNROLL - 1:
                                acc_done(l, KT - 1, 0, shift=KT * i)
                        product_lo(u, u % 2, A_UNROLL * i)
                    if ffn == 0:
                        mod_out(l, 0, i + 2, l, turn=i)
                for f in (FT - 2, FT - 1):
                    for j in range(2):
                        split_lo(l, c0 + 2 * (f + 1) + j)
                    q = q0 + 4 * (f - FT + 2)
                    mod_chunk(l, q)
                    mod_chunk(l, q + 1)
                    product(f, f % 2, 0)
                    mod_chunk(l, q + 2)
                    mod_chunk(l, q + 3)
                    if f == FT - 1:
                        acc_done(l, q + 3, 1)
                    product_lo(f, f % 2, 0)
                mod_out(l, q0 // KT, 7 + ffn, l)
                step = Chain(dve, dve_step, l, DVE_STEPS)
                step.n = steps[0]
                step(gates(l, 2 * ffn, 8 if ffn else 2, 0.5))
                steps[0] = step.n
                for n in range(KT):
                    for e in range(3 * n + AHEAD, 3 * n + AHEAD + 3):
                        split_lo(l, c0 + 2 * FT + e)
                    if ffn == 1:
                        for q in (2 * n, 2 * n + 1):
                            mod_chunk(l, q0 + KT + q)
                        if n % 4 == 3:
                            acc_done(l, q0 + KT + 2 * n + 1, 2)
                    update(l, 2 * ffn, n)
                    if ffn == 1 and n % 4 == 3:
                        mod_out(l, q0 // KT + 1 + n // 4, n // 4, (l + 1) % DEPTH)

            def cmul(step, o, p, q, t):
                step(V.tensor_tensor(o[0], p[0], q[0], ALU.mult), V.tensor_tensor(t, p[1], q[1], ALU.mult))
                step(V.tensor_tensor(o[0], o[0], t, ALU.subtract), V.tensor_tensor(o[1], p[0], q[1], ALU.mult))
                step(V.tensor_tensor(t, p[1], q[0], ALU.mult))
                step(V.tensor_tensor(o[1], o[1], t, ALU.add))

            def s5_constants(l, step):
                T = lambda i: s5_t[:, i, :]
                wait(dve, s5_act, l, 1)
                ar, ai = s5_a[:, 0, :], s5_a[:, 1, :]
                step(V.tensor_tensor(T(2), ai, T(0), ALU.mult))
                V.tensor_tensor(T(1), ar, T(0), ALU.mult).then_inc(s5_vec.sem, 1)
                reduce_angle(step, T(2), T(8), T(4))
                cos_angle(step, T(4), T(5))
                V.memset(T(9)[:, 0:1], 0.0).then_inc(s5_vec.sem, 1)
                wait(dve, s5_act, l, 4)
                sn, cs, mag = T(6), T(7), T(3)
                one = (pw[:, 0, 0, :], pw[:, 1, 0, :])
                step(V.memset(one[0], 1.0), V.memset(one[1], 0.0),
                     V.tensor_tensor(pw[:, 0, 1, :], mag, cs, ALU.mult),
                     V.tensor_tensor(pw[:, 1, 1, :], mag, sn, ALU.mult))
                step_p = 1
                t4 = s5_t[:, 8:12, :]
                while step_p < L:
                    top = [pw[:, z, step_p:step_p + 1, :].broadcast_to((P, step_p, NQ)) for z in range(2)]
                    cmul(step, [pw[:, z, step_p + 1:2 * step_p + 1, :] for z in range(2)],
                         [pw[:, z, 1:step_p + 1, :] for z in range(2)], top, t4[:, 0:step_p, :])
                    step_p *= 2
                cur = (cs, sn)
                spare = [(T(8), T(9)), (T(10), T(11))]
                for k in range(3 + 5):
                    nxt = (en[:, 0, k - 2, :], en[:, 1, k - 2, :]) if k >= 2 else spare[k % 2]
                    step(V.tensor_tensor(nxt[0], cur[0], cur[0], ALU.mult), V.tensor_tensor(T(12), cur[1], cur[1], ALU.mult),
                         V.scalar_tensor_tensor(out=nxt[1], in0=cur[0], scalar=2.0, in1=cur[1], op0=ALU.mult, op1=ALU.mult))
                    step(V.tensor_tensor(nxt[0], nxt[0], T(12), ALU.subtract))
                    cur = nxt
                step(V.tensor_tensor(T(8), ar, ar, ALU.mult), V.tensor_tensor(T(9), ai, ai, ALU.mult),
                     V.tensor_scalar(T(10), pw[:, 0, 1, :], 1.0, None, ALU.subtract))
                step(V.tensor_tensor(T(8), T(8), T(9), ALU.add))
                step(V.reciprocal(T(8), T(8)))
                nr, ni = T(10), pw[:, 1, 1, :]
                step(V.tensor_tensor(T(9), nr, ar, ALU.mult), V.tensor_tensor(T(11), ni, ai, ALU.mult),
                     V.tensor_tensor(T(12), nr, ai, ALU.mult))
                step(V.tensor_tensor(T(9), T(9), T(11), ALU.add), V.tensor_tensor(T(7), ni, ar, ALU.mult))
                step(V.tensor_tensor(T(7), T(7), T(12), ALU.subtract))
                step(V.tensor_tensor(fz[:, 0, :], T(9), T(8), ALU.mult), V.tensor_tensor(fz[:, 1, :], T(7), T(8), ALU.mult))

            def mixer_dve(l, step):
                m0 = MIX_BASE

                def rope(r):
                    dst = (qi_t[:, 0, :], qi_t[:, 1, :], ki_t[:], k_t[:], *(q_t[:, i, :] for i in range(AT)))[r]
                    wait(dve, swap_mm, l, r)
                    src = ps[:, 2, :] if r in (2, 3) else z_t[:, r % 2, :]
                    step(V.tensor_tensor(tmp_b[:, 0, :], src, rope_c[:], ALU.mult),
                         V.tensor_tensor(tmp_b[:, 1, :], ps[:, 3, :], rope_s[:], ALU.mult))
                    V.tensor_tensor(dst, tmp_b[:, 0, :], tmp_b[:, 1, :], ALU.add).then_inc(rope_done.sem, 1)
                    wait(dve, rope_done, l, r)

                def b_bar():
                    dve.wait_ge(mix_in.sem, mix_in.per * (l + 1))
                    f = [fz[:, z, :].rearrange("p (m i) -> p m i", i=GI).unsqueeze(3).broadcast_to((P, 4, GI, GC)) for z in range(2)]
                    b = [b_raw[:, z].rearrange("p m (i c) -> p m i c", i=GI) for z in range(2)]
                    o = [bb[:, z].rearrange("p m (i c) -> p m i c", i=GI) for z in range(2)]
                    cmul(step, o, b, f, tmp_b[:, 0, 0:4 * GI * GC].rearrange("p (m i c) -> p m i c", m=4, i=GI))
                    step(*(V.tensor_copy(pr[:, :, s, :], pw[:, :, L - 1 - s, :]) for s in range(L)))
                    step(V.memset(hs[:, :, :, 0:1], 0.0))
                    V.memset(dtmp[:, 0, 0:1], 0.0).then_inc(bb_done.sem, 1)

                def index_acc(n):
                    b, h = n // IDX_HEADS + 1, n % IDX_HEADS
                    w = (b + 1) * P
                    wait(dve, idx_relu, l, n)
                    dst, w_h = score[b], wi_n[:, b, h:h + 1]
                    if h == 0:
                        i = V.tensor_scalar(dst, tmp_a[:, n % 2, 0:w], w_h, None, ALU.mult)
                    else:
                        i = V.scalar_tensor_tensor(out=dst, in0=tmp_a[:, n % 2, 0:w], scalar=w_h, in1=dst, op0=ALU.mult, op1=ALU.add)
                    i.then_inc(idx_acc.sem, 1)
                    wait(dve, idx_acc, l, n)

                def topk_start(b):
                    step(V.memset(score[b][0:64, (b + 1) * P - 64:(b + 1) * P], INADM))

                def topk_round(b):
                    s = score[b]
                    settle(dve)
                    step(V.max(top8[:], s))
                    settle(dve)
                    step(V.match_replace(out=s, in_to_replace=top8[:], in_values=s, imm_value=TAKEN))

                def topk_end(b):
                    s = score[b]
                    V.tensor_scalar(s, s, -3.2e38, NEG, ALU.is_gt, ALU.mult).then_inc(mask_done.sem, 1)
                    wait(dve, mask_done, l, b)

                def mask0():
                    step(V.memset(score[0], 0.0))
                    V.memset(score[0][0:64, 64:P], NEG).then_inc(mask_done.sem, 1)
                    wait(dve, mask_done, l, 0)

                def mask_head(e):
                    b = e // HEADS
                    w = (b + 1) * P
                    wait(dve, logit, l, e)
                    if e >= 2:
                        wait(dve, p_exp, l, e - 2)
                        wait(dve, masked, l, e - 1)
                    settle(dve)
                    V.tensor_tensor_reduce(tmp_a[:, e % 2, 0:w], ps[:, e % 2, 0:w], score[b], -ATT_SCALE, 3.4e38,
                                           ALU.add, ALU.min, nmax[:, e % 2:e % 2 + 1]).then_inc(masked.sem, 1)

                def att_out(b):
                    wait(dve, pv, l, b * HEADS + HEADS - 1)
                    wait(dve, p_exp, l, b * HEADS + HEADS - 1)
                    step(V.reciprocal(rinv[:], rsum[:]))
                    V.tensor_tensor(att[:], ps[:, 3, :].rearrange("p (h d) -> p h d", d=HD),
                                    rinv[:].unsqueeze(2).broadcast_to((P, HEADS, HD)), ALU.mult).then_inc(att_n.sem, 1)
                    wait(dve, att_sq, l, b)
                    V.tensor_scalar(att_ss[:, 1:2], att_ss[:, 0:1], 1.0 / SW, EPS, ALU.mult, ALU.add).then_inc(att_ms.sem, 1)
                    wait(dve, att_rs, l, b)
                    V.tensor_scalar(att[:], att[:], att_ss[:, 2:3], None, ALU.mult).then_inc(att_sc.sem, 1)
                    wait(dve, att_tr, l, b)
                    V.tensor_tensor(tmp_b[:, 1, :].rearrange("p (m t) -> p m t", m=AT),
                                    ps[:, 2, :].rearrange("p (m t) -> p m t", m=AT),
                                    vcols[:, ds(56 + AT * l, AT)].unsqueeze(2).broadcast_to((P, AT, P)), ALU.mult).then_inc(att_f.sem, 1)
                    wait(dve, att_hi, l, b)
                    V.tensor_tensor(h_lo[:, 0:AT, b * P:(b + 1) * P], tmp_b[:, 1, :].rearrange("p (m t) -> p m t", m=AT),
                                    h_hi[:, 0:AT, b * P:(b + 1) * P].bitcast(F32), ALU.subtract).then_inc(att_done.sem, 1)
                    wait(dve, att_done, l, b)

                def s5_d(m):
                    wait(dve, kk_copy, l, 2 * m + 1)
                    kk = kk_y[0:GC, :].rearrange("c (g n) -> c g n", g=2 * GI)[:, :, 0:GC]
                    step(V.tensor_tensor(dtmp[:], ident[0:GC, 0:GC].unsqueeze(1).broadcast_to((GC, 2 * GI, GC)),
                                         d_raw[:, 2 * GI * m:2 * GI * (m + 1)].unsqueeze(2).broadcast_to((GC, 2 * GI, GC)), ALU.mult))
                    V.tensor_tensor(kk, kk, dtmp[:], ALU.add).then_inc(kk_d.sem, 1)
                    wait(dve, kk_d, l, m)

                def s5_scan(m):
                    wait(dve, st_mm, l, m)
                    S = [ps[:, 6 + z, 0:GI * J].rearrange("p (i j) -> p i j", i=GI) for z in range(2)]
                    E = [rot[:, m % 2, z] for z in range(2)]
                    X = [xr[:, z] for z in range(2)]
                    Gs = [gr[:, z] for z in range(2)]
                    M = [s5_m[:, z] for z in range(2)]
                    step(V.tensor_tensor(X[0], E[0], S[0], ALU.mult), V.tensor_tensor(M[0], E[1], S[1], ALU.mult),
                         V.tensor_tensor(X[1], E[0], S[1], ALU.mult), V.tensor_tensor(M[1], E[1], S[0], ALU.mult))
                    step(V.tensor_tensor(X[0], X[0], M[0], ALU.add), V.tensor_tensor(X[1], X[1], M[1], ALU.subtract))
                    flat = lambda v: v.rearrange("p i j -> p (i j)")
                    step(*(V.tensor_tensor_scan(flat(Gs[z]), flat(dec[:, m % 2]), flat(X[z]), 0.0, ALU.mult, ALU.add) for z in range(2)))
                    step(V.tensor_tensor(X[0], E[0], Gs[0], ALU.mult), V.tensor_tensor(M[0], E[1], Gs[1], ALU.mult),
                         V.tensor_tensor(X[1], E[0], Gs[1], ALU.mult), V.tensor_tensor(M[1], E[1], Gs[0], ALU.mult))
                    if m:
                        wait(dve, y_mm, l, m - 1)
                    step(V.tensor_tensor(hs[:, 0, :, 1:J + 1], X[0], M[0], ALU.subtract))
                    V.tensor_tensor(hs[:, 1, :, 1:J + 1], X[1], M[1], ALU.add).then_inc(hs_done.sem, 1)
                    wait(dve, hs_done, l, m)

                def s5_lo(m):
                    wait(dve, y_act, l, 2 * m + 1)
                    V.tensor_tensor(h_lo[:, AT + m, :], z_t[:, 0, :], h_hi[:, AT + m, :].bitcast(F32), ALU.subtract).then_inc(y_done.sem, 1)

                for t in range(12):
                    split_lo(l, m0 + t + AHEAD)
                    if t == 2:
                        rope(0)
                    if t == 3:
                        rope(1)
                        b_bar()
                    if t == 4:
                        rope(2)
                        rope(3)
                        mask0()
                    if t >= 6 and t <= 9:
                        rope(t - 2)
                    if t == 6:
                        wait(dve, v_done, l, 1)
                    if t in (6, 7, 8):
                        for n in range(IDX_HEADS):
                            index_acc((t - 6) * IDX_HEADS + n)
                        topk_start(t - 5)
                for _ in range(TOPK // 8):
                    topk_round(1)
                topk_end(1)
                for b in range(QB):
                    for h in range(HEADS):
                        mask_head(b * HEADS + h)
                        if b in (0, 1):
                            topk_round(b + 2)
                            topk_round(b + 2)
                        if h == 0:
                            s5_d(b)
                        if h == 5:
                            s5_scan(b)
                    if b in (0, 1):
                        topk_end(b + 2)
                    att_out(b)
                    s5_lo(b)
                for n in range(ST):
                    split_lo(l, m0 + 12 + n + AHEAD)
                for n in range(ST):
                    wait(dve, glu_act, l, n)
                    step(V.tensor_scalar(tmp_a[:, n % 2, :], tmp_a[:, n % 2, :], 0.5, 0.5, ALU.mult, ALU.add))
                    if n == 0:
                        used(dve, l, m0 + 12 + ST - 1)
                    step(V.tensor_tensor(q_t[:, n, :], h_hi[:, AT + n, :].bitcast(F32), h_lo[:, AT + n, :].bitcast(F32), ALU.add))
                    V.tensor_tensor(q_t[:, n, :], q_t[:, n, :], tmp_a[:, n % 2, :], ALU.mult).then_inc(ssm_y.sem, 1)
                wait(dve, ssm_ss, l, ST - 1)
                rms(l, 2, SW, step)
                wait(dve, bcast, l, 2)
                wait(dve, ssm_y, l, ST - 1)
                for n in range(ST):
                    if n >= 2:
                        wait(dve, mix_done, l, n - 2)
                    V.scalar_tensor_tensor(out=tmp_a[:, n % 2, :], in0=q_t[:, n, :], scalar=vcols[:, ds(64 + ST * l + n, 1)],
                                           in1=ps[:, 7, :], op0=ALU.mult, op1=ALU.mult).then_inc(ssm_f.sem, 1)
                    wait(dve, ssm_hi, l, n)
                    V.tensor_tensor(h_lo[:, AT + n, :], tmp_a[:, n % 2, :], h_hi[:, AT + n, :].bitcast(F32), ALU.subtract).then_inc(mix_done.sem, 1)
                for n in range(KT):
                    split_lo(l, m0 + 16 + n + AHEAD)
                    update(l, 1, n)

            steps = [0]
            with dve.Fori(0, DEPTH) as l:
                steps[0] = 0

                def chain():
                    c = Chain(dve, dve_step, l, DVE_STEPS)
                    c.n = steps[0]
                    return c

                step = chain()
                norm(l, 0, 0, 1, 0, 2, 0.5, step)
                s5_constants(l, step)
                steps[0] = step.n
                ffn_dve(l, 0)
                step = chain()
                step(gates(l, 1, 5, 1.0), V.tensor_scalar(half_bias[:], vcols[:, ds(72 + ST * l, ST)], 0.5, None, ALU.mult))
                norm(l, 1, 1, 4, 3, 5, 1.0, step)
                mixer_dve(l, step)
                norm(l, 2, 3, 7, 6, 8, 0.5, step)
                steps[0] = step.n
                ffn_dve(l, 1)
                assert steps[0] == DVE_STEPS, steps[0]

            wait(dve, ssq, DEPTH, -1)
            rms(DEPTH, 0, D, None)
            wait(dve, bcast, DEPTH, 0)
            for n in range(KT):
                if n >= 2:
                    dve.wait_ge(out_tr, n - 1)
                V.scalar_tensor_tensor(out=o_t[:, n % 2, :], in0=x[:, n, :], scalar=vcols[:, 48 + n:49 + n], in1=ps[:, 7, :],
                                       op0=ALU.mult, op1=ALU.mult).then_inc(out_f, 1)

        @block.gpsimd
        def _(pool):
            Q = nc.gpsimd

            def power(layer, idx):
                wait(pool, ms_ready, layer, idx)
                Q.tensor_tensor(rstd[:], ms[:], mhalf[:], ALU.pow).then_inc(rstd_ready.sem, 1)

            def cmul(step, o, p, q, t, p0n=None):
                step(Q.tensor_tensor(o[0], p[0], q[0], ALU.mult), Q.tensor_tensor(t, p[1], q[1], ALU.mult))
                step(Q.tensor_tensor(o[0], o[0], t, ALU.subtract))
                step(Q.tensor_tensor(o[1], p[0] if p0n is None else p0n, q[1], ALU.mult), Q.tensor_tensor(t, p[1], q[0], ALU.mult))
                step(Q.tensor_tensor(o[1], o[1], t, ALU.add if p0n is None else ALU.subtract))

            def s5_prep(l, m, step):
                if m >= 2:
                    wait(pool, y_mm, l, m - 2)
                n9, n8 = (P, GI, L + 1, GC), (P, GI, L, GC)
                c3 = [ct[:, z, m, :].rearrange("p (i c) -> p i c", i=GI).unsqueeze(2).broadcast_to(n9) for z in range(3)]
                q9 = [pw[:, z, :, m * GI:(m + 1) * GI].rearrange("p t i -> p i t").unsqueeze(3).broadcast_to(n9) for z in range(2)]
                cmul(step, [ca[:, m % 2, z] for z in range(2)], c3[0:2], q9,
                     pool_t[:].rearrange("p (i t c) -> p i t c", i=GI, c=GC), p0n=c3[2])
                if m >= 1:
                    wait(pool, w_tr, l, m - 1)
                b2 = [bb[:, z, m, :].rearrange("p (i c) -> p i c", i=GI).unsqueeze(2).broadcast_to(n8) for z in range(2)]
                q8 = [pr[:, z, :, m * GI:(m + 1) * GI].rearrange("p t i -> p i t").unsqueeze(3).broadcast_to(n8) for z in range(2)]
                cmul(step, [ab[:, z] for z in range(2)], b2, q8,
                     pool_t[:, 0:GI * L * GC].rearrange("p (i t c) -> p i t c", i=GI, c=GC))
                r = [rot[:, m % 2, z] for z in range(2)]
                settle(pool)
                step(Q.memset(r[0][:, :, 0:1], 1.0), Q.memset(r[1][:, :, 0:1], 0.0),
                     Q.memset(dec[:, m % 2, :, 0:1], 0.0),
                     Q.tensor_copy(dec[:, m % 2, :, 1:J], mag_l[:, m * GI:(m + 1) * GI].unsqueeze(2).broadcast_to((P, GI, J - 1))))
                for k in range(6):
                    n = 1 << k
                    e = [en[:, z, k, m * GI:(m + 1) * GI].unsqueeze(2).broadcast_to((P, GI, n)) for z in range(2)]
                    cmul(step, [r[z][:, :, n:2 * n] for z in range(2)], [r[z][:, :, 0:n] for z in range(2)], e,
                         pool_t[:, 0:GI * n].rearrange("p (i j) -> p i j", i=GI))
                settle(pool)
                Q.memset(pool_t[:, 0:1], 0.0).then_inc(prep.sem, 1)
                wait(pool, prep, l, m)

            pool.wait_ge(credits, 3)
            with pool.Fori(0, DEPTH) as l:
                step = Chain(pool, pool_step, l, POOL_STEPS)
                power(l, 0)
                power(l, 1)
                projected(pool, l, KT - 1)
                settle(pool)
                Q.memset(toep[:], 0.0).then_inc(toep0.sem, 1)
                wait(pool, ct_done, l, 2)
                wait(pool, bb_done, l, 0)

                def att_power(b):
                    wait(pool, att_ms, l, b)
                    Q.tensor_tensor(att_ss[:, 2:3], att_ss[:, 1:2], mhalf[:, 0:1], ALU.pow).then_inc(att_rs.sem, 1)

                s5_prep(l, 0, step)
                s5_prep(l, 1, step)
                att_power(0)
                s5_prep(l, 2, step)
                att_power(1)
                s5_prep(l, 3, step)
                att_power(2)
                att_power(3)
                power(l, 2)
                power(l, 3)
                assert step.n == POOL_STEPS, step.n
            power(DEPTH, 0)

        @block.tensor
        def _(pe):
            mm = nc.tensor.matmul

            def split3(out, w, rhs_hi, rhs_lo, first, last):
                hi, lo = w
                mm(out, hi, rhs_hi, start=first, stop=False)
                mm(out, hi, rhs_lo, start=False, stop=False)
                return mm(out, lo, rhs_hi, start=False, stop=last)

            def w_tile(c, k):
                s = slice(k * P, (k + 1) * P)
                return w_hi[:, c % RING, s], w_lo[:, c % RING, s]

            def chunk_ready(layer, c, shift=0):
                pe.wait_ge(w_split_lo.sem, w_split_lo.after(layer, c) + shift)

            def mod_sum(layer, j, turn=0):
                pe.wait_ge(acc_ready.sem, acc_ready.after(layer, j) + turn)
                pe.wait_ge(mod_done.sem, mod_done.after(layer, j - 1) + turn)
                for k in range(KT):
                    i = mm(ps[:, 7, k:k + 1], mod_acc[:, k * P:(k + 1) * P], ones[:, 0:1], start=True, stop=True)
                i.then_inc(mod_psum.sem, 1)

            def squares_sum(layer, e, buf, done, src, last_k, k):
                wait(pe, done, layer, e)
                for b in range(QB):
                    i = mm(ps[:, 6, b:b + 1], tmp_b[:, buf, b * P:(b + 1) * P], ones[:, 0:1],
                           start=(k == 0 and b == 0), stop=(k == last_k), skip_group_check=True)
                i.then_inc(src.sem, 1)

            def rms_bcast(layer, idx):
                wait(pe, diag_ready, layer, idx)
                mm(ps[:, 7, :], ones[:], tmp_b[:, 0, :], start=True, stop=True).then_inc(bcast.sem, 1)

            pe.wait_ge(in_const, 32)
            pe.wait_ge(in_c, 96)
            nc.tensor.transpose(ps[:, 4, 0:88], vraw[0:88, 0, :], ident[0:88, 0:88]).then_inc(prologue, 1)
            pe.wait_ge(in_vec, 32)
            for l in range(DEPTH):
                nc.tensor.transpose(ps[:, 5, l * P:l * P + 72], vraw[0:72, 1 + l, :], ident[0:72, 0:72]).then_inc(prologue, 1)
            pe.wait_ge(credits, 6)
            for j in range(2):
                pe.wait_ge(acc_ready.sem, j + 1)
                if j:
                    pe.wait_ge(mod_done.sem, j)
                for k in range(KT):
                    i = mm(ps[:, 7, k:k + 1], mod_acc[:, k * P:(k + 1) * P], ones[:, 0:1], start=True, stop=True)
                i.then_inc(mod_psum.sem, 1)
            pe.wait_ge(in_x, 16)
            for n in range(KT + 1):
                if n < KT:
                    wait(pe, x_new, 0, n - KT - 2)
                    for b in range(QB):
                        i = nc.tensor.transpose(ps[:, 4 + n % 2, b * P:(b + 1) * P], x_in[:, b, n * P:(n + 1) * P], ident[:])
                    i.then_inc(prologue, 1)
                if n:
                    squares_sum(0, n - 1 - KT, (n - 1) % 2, sq_done, ssq, KT - 1, n - 1)

            def ffn_pe(l, ffn):
                c0, f0 = FFN_BASE[ffn], ffn * FT

                rms_bcast(l, 3 * ffn)
                if ffn == 0:
                    s5_select(l)
                with pe.Fori(0, A_TURNS) as i:
                    for u in range(A_UNROLL):
                        tile_pe(l, ffn, u, u % 2, A_UNROLL * i, 2 * A_UNROLL * i, u == 0)
                    if ffn == 0:
                        mod_sum(l, 0, turn=i)
                for f in (FT - 2, FT - 1):
                    tile_pe(l, ffn, f, f % 2, 0, 0, False)
                mod_sum(l, A_TURNS + ffn)
                wait(pe, g_done, l, f0 + FT - 1)
                for n in range(KT + 1):
                    e = 2 * ffn * KT + n
                    if n < KT:
                        wait(pe, x_new, l, e - 2)
                        for j in range(3):
                            c = c0 + 2 * FT + 3 * n + j
                            chunk_ready(l, c)
                            k0, kn = down_chunk(j)
                            for k in range(kn):
                                i = split3(ps[:, 4 + n % 2, :], w_tile(c, k), g_hi[:, k0 + k, :], g_lo[:, k0 + k, :],
                                           k0 + k == 0, k0 + k == FT - 1)
                            i.then_inc(w_used.sem, 1)
                        if ffn == 1 and n % 4 == 3:
                            mod_sum(l, A_TURNS + 2 + n // 4)
                    if n:
                        squares_sum(l, e - 1, (n - 1) % 2, sq_done, ssq, KT - 1, n - 1)

            def tile_pe(l, ffn, f, parity, shift, cshift, by_k):
                c, f0 = FFN_BASE[ffn] + 2 * f, ffn * FT
                pe.wait_ge(w_split_lo.sem, w_split_lo.after(l, c + 1) + cshift)
                pe.wait_ge(g_full.sem, g_full.after(l, f0 + f - 2) + shift)
                for k in range(KT):
                    if by_k:
                        wait(pe, h_done, l, 2 * ffn * KT + k)
                    for z in range(2):
                        i = split3(ps[:, 2 * parity + z, :], w_tile(c + z, k), h_hi[:, k, :], h_lo[:, k, :], k == 0, k == KT - 1)
                        if k == KT - 1:
                            i.then_inc(w_used.sem, 1)

            def s5_select(l):
                pe.wait_ge(s5_in.sem, 64 * l + 64)
                sel = ident[0:G, 0:G].rearrange("g (m t i) -> g t m i", t=2, i=GI)
                for z in range(2):
                    for g2 in range(2):
                        i = mm(ps[g2 * NS:(g2 + 1) * NS, 6, 16 + z * NQ:16 + (z + 1) * NQ], s5_raw[:, z, :], sel[:, g2],
                               start=True, stop=True)
                i.then_inc(s5_sel.sem, 1)

            def mixer_pe(l):
                m0 = MIX_BASE

                def project(t):
                    c = m0 + t
                    chunk_ready(l, c)
                    if t >= 2:
                        wait(pe, z_copy, l, t - 2)
                    for k in range(KT):
                        if t == 0:
                            wait(pe, h_done, l, KT + k)
                        i = split3(ps[:, t % 2, :], w_tile(c, k), h_hi[:, k, :], h_lo[:, k, :], k == 0, k == KT - 1)
                    i.then_inc(w_used.sem, 1)

                def swap(r, t, first, second):
                    wait(pe, z_copy, l, t)
                    if r:
                        wait(pe, rope_done, l, r - 1)
                    if first is not None:
                        mm(ps[:, 2, :], swaps[:, first, :], z_t[:, t % 2, :], start=True, stop=True)
                    mm(ps[:, 3, :], swaps[:, second, :], z_t[:, t % 2, :], start=True, stop=True).then_inc(swap_mm.sem, 1)

                def index(n):
                    b, h = n // IDX_HEADS + 1, n % IDX_HEADS
                    r = slice(h % 2 * HD, h % 2 * HD + HD)
                    if n >= 2:
                        wait(pe, idx_relu, l, n - 2)
                    mm(ps[:, 4 + n % 2, 0:(b + 1) * P], qi_t[r, h // 2, b * P:(b + 1) * P], ki_t[r, 0:(b + 1) * P],
                       start=True, stop=True).then_inc(idx_mm.sem, 1)

                def logits(e):
                    b, h = e // HEADS, e % HEADS
                    r = slice(h % 2 * HD, h % 2 * HD + HD)
                    if e >= 2:
                        wait(pe, masked, l, e - 2)
                    mm(ps[:, e % 2, 0:(b + 1) * P], q_t[r, h // 2, b * P:(b + 1) * P], k_t[r, 0:(b + 1) * P],
                       start=True, stop=True).then_inc(logit.sem, 1)

                def turn(e):
                    b = e // HEADS
                    wait(pe, p_exp, l, e)
                    if e:
                        wait(pe, pt_copy, l, e - 1)
                    if e % HEADS == 0 and b:
                        wait(pe, att_f, l, b - 1)
                    for s in range(b + 1):
                        i = nc.tensor.transpose(ps[:, 2, s * P:(s + 1) * P], tmp_b[:, e % 2, s * P:(s + 1) * P], ident[:])
                    i.then_inc(pt_mm.sem, 1)

                def values(e):
                    b, h = e // HEADS, e % HEADS
                    wait(pe, pt_copy, l, e)
                    if h == 0 and b:
                        wait(pe, att_n, l, b - 1)
                    for s in range(b + 1):
                        i = mm(ps[:, 3, h * HD:(h + 1) * HD], pt[:, e % 2, s * P:(s + 1) * P], v_n[:, s, :],
                               start=(s == 0), stop=(s == b))
                    i.then_inc(pv.sem, 1)

                def att_turn(b):
                    wait(pe, att_sc, l, b)
                    for m in range(AT):
                        i = nc.tensor.transpose(ps[:, 2, m * P:(m + 1) * P], att[:, 2 * m:2 * m + 2, :].rearrange("p h d -> p (h d)"), ident[:])
                    i.then_inc(att_tr.sem, 1)

                def halves(g):
                    return slice(g // GI * NS, (g // GI + 1) * NS), g % GI

                def s5_kk(m):
                    wait(pe, prep, l, m)
                    if m:
                        wait(pe, y_copy, l, 2 * m - 1)
                    settle(pe)
                    for g in range(2 * GI):
                        r, q = halves(g)
                        for z in range(2):
                            i = mm(ps[0:GC, 4 + g // GI, (g % GI) * P:(g % GI + 1) * P], bb[r, z, m, q * GC:(q + 1) * GC],
                                   ca[r, m % 2, z, q, 0:L, :].rearrange("p t c -> p (t c)"), start=(z == 0), stop=(z == 1))
                    i.then_inc(kk_mm.sem, 1)

                def s5_w(m):
                    wait(pe, kk_copy, l, 2 * m + 1)
                    for z in range(2):
                        for q in range(GI):
                            i = nc.tensor.transpose(ps[:, 4 + z, q * P:(q + 1) * P], ab[:, z, q].rearrange("p s c -> p (s c)"), ident[:])
                    i.then_inc(w_tr.sem, 1)

                def s5_un(m):
                    wait(pe, w_copy, l, 2 * m + 1)
                    settle(pe)
                    for s in range(L):
                        i = nc.tensor.transpose(ps[0:J, 4 + s // 4, (s % 4) * P:(s % 4 + 1) * P], u_t[:, m, s, :], ident[:])
                    i.then_inc(un_tr.sem, 1)

                def s5_u8(m):
                    wait(pe, un_copy, l, 2 * m + 1)
                    settle(pe)
                    for g in range(2 * GI):
                        i = nc.tensor.transpose(ps[:, 4, g * J:(g + 1) * J], un[:, g].rearrange("j s c -> j (s c)"), ident[0:J, 0:J])
                    i.then_inc(u8_tr.sem, 1)

                def s5_states(m):
                    wait(pe, u8_copy, l, m)
                    if m:
                        wait(pe, y_act, l, 2 * m - 2)
                    for z in range(2):
                        for g in range(2 * GI):
                            r, q = halves(g)
                            i = mm(ps[r, 6 + z, q * J:(q + 1) * J], wst[:, z, q, r], u8[:, g, :], start=True, stop=True)
                    i.then_inc(st_mm.sem, 1)

                def s5_y(m):
                    pe.wait_ge(toep_in.sem, toep_in.per * l + 16 * L * (m + 1))
                    wait(pe, hs_done, l, m)
                    for g in range(2 * GI):
                        r, q = halves(g)
                        out = ps[0:J, 4 + g // GI, (g % GI) * P:(g % GI + 1) * P]
                        mm(out, u8[:, g, :], toep[:, g, :], start=True, stop=False)
                        for z in range(2):
                            i = mm(out, hs[r, z, q, 0:J], ca[r, m % 2, z, q, 1:L + 1, :].rearrange("p t c -> p (t c)"),
                                   start=False, stop=(z == 1))
                    i.then_inc(y_mm.sem, 1)

                def s5_yt(m):
                    wait(pe, y_copy, l, 2 * m + 1)
                    settle(pe)
                    for t in range(L):
                        i = nc.tensor.transpose(ps[:, 6, t * J:(t + 1) * J], kk_y[:, t * P:(t + 1) * P], ident[0:J, 0:J])
                    i.then_inc(y_tr.sem, 1)

                rms_bcast(l, 1)
                pe.wait_ge(mix_in.sem, mix_in.per * (l + 1))
                for t in range(12):
                    project(t)
                    if t == 1:
                        settle(pe)
                        for z in range(2):
                            for m in range(4):
                                i = nc.tensor.transpose(ps[:, 7, z * 256 + m * 64:z * 256 + (m + 1) * 64], c_raw[:, z, m, :], ident[0:64, 0:64])
                        i.then_inc(ct_mm.sem, 1)
                    if t in (1, 2):
                        swap(t - 1, t - 1, None, 0)
                    if t == 3:
                        swap(2, 2, 3, 4)
                        swap(3, 2, 1, 2)
                    if t == 4:
                        wait(pe, z_copy, l, 3)
                        for b in range(QB):
                            i = nc.tensor.transpose(ps[:, 4, b * P:(b + 1) * P], z_t[:, 1, b * P:(b + 1) * P], ident[:])
                        i.then_inc(v_tr.sem, 1)
                    if 5 <= t <= 8:
                        swap(t - 1, t - 1, None, 0)
                    if t == 6:
                        wait(pe, v_done, l, 1)
                        wait(pe, rope_done, l, 3)
                    if t in (6, 7, 8):
                        for n in range(IDX_HEADS):
                            index((t - 6) * IDX_HEADS + n)
                wait(pe, z_copy, l, 11)
                wait(pe, idx_relu, l, 11)
                wait(pe, rope_done, l, 7)
                logits(0)
                for b in range(QB):
                    steps = {0: s5_kk, 1: s5_w, 2: s5_un, 3: s5_u8, 4: s5_states, 7: s5_y}
                    for h in range(HEADS):
                        e = b * HEADS + h
                        if e + 1 < NA:
                            logits(e + 1)
                        turn(e)
                        if h:
                            values(e - 1)
                        if h in steps:
                            steps[h](b)
                    values(b * HEADS + HEADS - 1)
                    att_turn(b)
                    s5_yt(b)
                wait(pe, att_f, l, QB - 1)
                wait(pe, y_done, l, 3)
                for n in range(ST):
                    c = m0 + 12 + n
                    chunk_ready(l, c)
                    for k in range(ST):
                        i = split3(ps[:, n, :], w_tile(c, k), h_hi[:, AT + k, :], h_lo[:, AT + k, :], k == 0, k == ST - 1)
                    i.then_inc(w_used.sem, 1)
                for n in range(ST):
                    squares_sum(l, n, n % 2, ssm_sq, ssm_ss, ST - 1, n)
                rms_bcast(l, 2)
                wait(pe, att_done, l, QB - 1)
                for n in range(KT + 1):
                    if n < KT:
                        c = m0 + 16 + n
                        chunk_ready(l, c)
                        wait(pe, x_new, l, KT + n - 2)
                        for k in range(KT):
                            if n == 0 and k >= AT:
                                wait(pe, mix_done, l, k - AT)
                            i = split3(ps[:, 4 + n % 2, :], w_tile(c, k), h_hi[:, k, :], h_lo[:, k, :], k == 0, k == KT - 1)
                        i.then_inc(w_used.sem, 1)
                    if n:
                        squares_sum(l, KT + n - 1, (n - 1) % 2, sq_done, ssq, KT - 1, n - 1)

            with pe.Fori(0, DEPTH) as l:
                ffn_pe(l, 0)
                mixer_pe(l)
                ffn_pe(l, 1)

            rms_bcast(DEPTH, 0)
            for n in range(KT):
                pe.wait_ge(out_f, n + 1)
                if n >= 2:
                    pe.wait_ge(out_copy, n - 1)
                for b in range(QB):
                    i = nc.tensor.transpose(ps[:, 4 + n % 2, b * P:(b + 1) * P], o_t[:, n % 2, b * P:(b + 1) * P], ident[:])
                i.then_inc(out_tr, 1)



_INS = ["x", "c", "positions", "mod_w", "mod_b", "norm_g", "ffn1_w1", "ffn1_w3", "ffn1_w2", "ffn2_w1", "ffn2_w3",
        "ffn2_w2", "w_in", "w_out", "attn_gain", "ssm_gain", "ssm_a_re", "ssm_a_im", "ssm_log_dt", "ssm_b_re",
        "ssm_b_im", "ssm_c_re", "ssm_c_im", "ssm_d", "glu_w", "glu_b", "final_g"]


def kernel(**inputs):
    import concourse.bacc as bacc
    from concourse.bass_utils import run_bass_kernel_spmd

    nc = bacc.Bacc("TRN2", target_bir_lowering=False, num_devices=1, dynamic_dma_scratch_size=1024)
    arrays = {f"in_{n}": np.ascontiguousarray(inputs[n]) for n in _INS}
    arrays["in_consts"] = shape_constants()
    a = {n[3:]: nc.dram_tensor(n, v.shape, mybir.dt.from_np(v.dtype), kind="ExternalInput").ap() for n, v in arrays.items()}
    a["out"] = nc.dram_tensor("out", (1, SEQ, D), F32, kind="ExternalOutput").ap()
    trunk(nc, a)
    r = run_bass_kernel_spmd(nc, [arrays], core_ids=[0])
    return r.results[0]["out"]
```

```python
from contextlib import ExitStack

import numpy as np

import concourse.bass as bass
from concourse import mybir

F32 = mybir.dt.float32
F32R = mybir.dt.float32r
I32 = mybir.dt.int32
ALU = mybir.AluOpType
ACT = mybir.ActivationFunctionType
ds = bass.ds

P = 128
DEPTH = 2
D = 1024
KT = D // P
SEQ = 512
QB = SEQ // P
F = 2816
FT = F // P
HEADS = 8
HD = 64
AT = HEADS * HD // P
IDX_HEADS = 4
TOPK = 128
SW = 512
ST = SW // P
G = 32
GC = 16
NS = 64
L = 8
J = SEQ // L
GI = 4
N_MOD = 9
EPS = 1e-6
ATT_SCALE = HD ** -0.5
IDX_SCALE = HD ** -0.5 * IDX_HEADS ** -0.5
ROT = HD // 4
INV_FREQ = (1, 0.193922758, 0.0376060307, 0.00729266508, 0.00141421345,
            0.000274248188, 5.31829573e-05, 1.03133852e-05)
COL_K, COL_KI, COL_QI, COL_U = 512, 896, 640, 964
NEG = -1.0e30
INADM = -3.0e38
TAKEN = -3.4e38
TWO_PI_A, TWO_PI_B, TWO_PI_C = 6.28125, 0.0019350051879882812, 3.019915981956753e-07
INV_2PI = 0.15915494309189535
ROUND = 12582912.0
HALF_PI = 1.5707963267948966

RING = 4
MIX_FIRST = 6
AHEAD = 2
DOWN_K = (8, 8, 6)
FFN_CHUNKS = 2 * FT + KT * len(DOWN_K)
MIX_CHUNKS = 8 + ST + ST + KT
FFN_BASE = (0, FFN_CHUNKS + MIX_CHUNKS)
MIX_BASE = FFN_CHUNKS
LAYER_CHUNKS = 2 * FFN_CHUNKS + MIX_CHUNKS
assert LAYER_CHUNKS % RING == 0
A_UNROLL = 4
A_TURNS = (FT - 2) // A_UNROLL
MOD_RING = 4
S5_LEAD = 4
MOD_TURN = ((0, 1, 2), (3, 4, 5), (6, 7), ())
MOD_REST = ((0, 1, 2, 3, 4), (5, 6, 7))
FIRST_MODS = 4
DVE_STEPS, POOL_STEPS = 273, 208

C_ID, C_SWAP, C_RK, C_SRK, C_RKI, C_SRKI = (i * P for i in range(6))
C_COLS = 6 * P


def shape_constants():
    t = np.zeros((P, 6 * P + 4), np.float32)
    m = np.arange(P)
    d = m % HD
    other = np.where(d < ROT // 2, m + ROT // 2, np.where(d < ROT, m - ROT // 2, m))
    rot = d < ROT
    t[m, C_ID + m] = 1.0
    t[other[rot], C_SWAP + m[rot]] = 1.0
    t[d, C_RK + m] = 1.0
    t[(other % HD)[rot], C_SRK + m[rot]] = 1.0
    t[d + HD, C_RKI + m] = 1.0
    t[(other % HD + HD)[rot], C_SRKI + m[rot]] = 1.0
    freq = np.array(INV_FREQ, np.float32)
    t[:, C_COLS] = np.where(rot, freq[d % (ROT // 2)], 0.0)
    t[:, C_COLS + 1] = np.where(rot, np.where(d < ROT // 2, -1.0, 1.0), 0.0)
    t[:, C_COLS + 2] = rot
    t[:, C_COLS + 3] = ~rot
    return t


class Signal:

    def __init__(self, sem, per, start=0):
        self.sem, self.per, self.start = sem, per, start

    def after(self, layer, k):
        return layer * self.per + (self.start + k + 1)


class Chain:

    def __init__(self, eng, sem, layer, per):
        self.eng, self.sem, self.base, self.n = eng, sem, layer * per, 0

    def __call__(self, *instructions):
        for i in instructions:
            i.then_inc(self.sem, 1)
            self.n += 1
        self.eng.wait_ge(self.sem, self.base + self.n)


def trunk(nc, a):
    ctx = ExitStack()
    with ctx:
        def sb(name, shape, dt=F32, at=None):
            return (at or ctx).enter_context(nc.sbuf_tensor(name, shape, dt))

        def sem(name):
            return ctx.enter_context(nc.semaphore(name))

        x = sb("x", [P, KT, SEQ])
        h_hi = sb("h_hi", [P, KT, SEQ], F32R)
        h_lo = sb("h_lo", [P, KT, SEQ], F32R)
        stage = sb("stage", [P, RING, 1024])
        w_hi = sb("w_hi", [P, RING, 1024], F32R)
        w_lo = sb("w_lo", [P, RING, 1024], F32R)
        mod_stage = sb("mod_stage", [P, MOD_RING, D])
        mod_acc = sb("mod_acc", [P, D])
        tmp_a = sb("tmp_a", [P, 2, SEQ])
        tmp_b = sb("tmp_b", [P, 2, SEQ])
        rope_c = sb("rope_c", [P, SEQ])
        rope_s = sb("rope_s", [P, SEQ])
        ident = sb("ident", [P, P])
        ones = sb("ones", [P, P])
        cols = sb("cols", [P, 4])
        vcols = sb("vcols", [P, 88])
        modb = sb("modb", [P, DEPTH * N_MOD * KT])
        modc = sb("modc", [P, N_MOD, KT])
        c_silu = sb("c_silu", [P, KT])
        a_col = sb("a_col", [P, KT])
        gate = sb("gate", [P, 3, KT])
        half_bias = sb("half_bias", [P, ST])
        half_gain = sb("half_gain", [P, ST])
        ms = sb("ms", [P, 4])
        rstd = sb("rstd", [P, 4])
        mhalf = sb("mhalf", [P, 4])
        NQ = 4 * GI
        s5_raw = sb("s5_raw", [G, 2, NS])
        s5_ldt = sb("s5_ldt", [P, NQ])
        s5_a = sb("s5_a", [P, 2, NQ])
        s5_t = sb("s5_t", [P, 14, NQ])
        pw = sb("pw", [P, 2, L + 1, NQ])
        en = sb("en", [P, 2, 6, NQ])
        fz = sb("fz", [P, 2, NQ])
        mag_l = sb("mag_l", [P, NQ])

        EARLY = ExitStack()
        x_in = sb("x_in", [P, QB, D], at=EARLY)
        vraw = sb("vraw", [P, 3, P], at=EARLY)
        pos_i = sb("pos_i", [P, SEQ], I32, at=EARLY)
        mod_acc_b = sb("mod_acc_b", [P, D], at=EARLY)
        mod_first = sb("mod_first", [P, 2, KT, D], at=EARLY)
        EARLY.close()
        FFN = ExitStack()
        g_hi = sb("g_hi", [P, FT, SEQ], F32R, at=FFN)
        g_lo = sb("g_lo", [P, FT, SEQ], F32R, at=FFN)
        FFN.close()
        MIX = ExitStack()
        q_t = sb("q_t", [P, AT, SEQ], at=MIX)
        k_t = sb("k_t", [P, SEQ], at=MIX)
        qi_t = sb("qi_t", [P, 2, SEQ], at=MIX)
        ki_t = sb("ki_t", [P, SEQ], at=MIX)
        z_t = sb("z_t", [P, 2, SEQ], at=MIX)
        u_t = sb("u_t", [P, ST, L, J], at=MIX)
        v_n = sb("v_n", [P, QB, HD], at=MIX)
        wi_n = sb("wi_n", [P, QB, IDX_HEADS], at=MIX)
        score_all = sb("score", [P, QB * (QB + 1) // 2 * P], at=MIX)
        score = [score_all[:, b * (b + 1) // 2 * P:(b + 1) * (b + 2) // 2 * P] for b in range(QB)]
        top8 = sb("top8", [P, 8], at=MIX)
        nmax = sb("nmax", [P, 2], at=MIX)
        rsum = sb("rsum", [P, 2, HEADS], at=MIX)
        rinv = sb("rinv", [P, HEADS], at=MIX)
        att_ss = sb("att_ss", [P, 3], at=MIX)
        pt = sb("pt", [P, 2, SEQ], at=MIX)
        att = sb("att", [P, HEADS, HD], at=MIX)
        d_raw = sb("d_raw", [GC, G], at=MIX)
        ct = sb("ct", [P, 3, 4, GI * GC], at=MIX)
        bb = sb("bb", [P, 2, 4, GI * GC], at=MIX)
        pr = sb("pr", [P, 2, L, NQ], at=MIX)
        ca = sb("ca", [P, 2, 2, GI, L + 1, GC], at=MIX)
        ab = sb("ab", [P, 2, GI, L, GC], at=MIX)
        rot = sb("rot", [P, 2, 2, GI, J], at=MIX)
        dec = sb("dec", [P, 2, GI, J], at=MIX)
        pool_t = sb("pool_t", [P, GI * (L + 1) * GC], at=MIX)
        wst = sb("wst", [P, 2, GI, P], at=MIX)
        toep = sb("toep", [P, 2 * GI, P], at=MIX)
        kk_y = sb("kk_y", [NS, 2 * GI * P], at=MIX)
        un = sb("un", [J, 2 * GI, L, GC], at=MIX)
        hs = sb("hs", [P, 2, GI, J + 1], at=MIX)
        dtmp = sb("dtmp", [GC, 2 * GI, GC], at=MIX)
        with ExitStack() as first_half:
            swaps = sb("swaps", [P, 5, P], at=first_half)
        u8 = sb("u8", [P, 2 * GI, J], at=MIX)
        MIX.close()
        ab = (ab, mod_acc[:].rearrange("p (z i s c) -> p z i s c", z=2, i=GI, s=L))
        c_raw = mod_stage[0:GI * GC, 0, :].rearrange("p (z m n) -> p z m n", z=2, m=4)
        b_raw = mod_stage[:, 1, 0:2 * 4 * GI * GC].rearrange("p (z m n) -> p z m n", z=2, m=4)
        xr, gr, s5_m = (mod_stage[:, 2 + i // 2, i % 2 * 512:i % 2 * 512 + 512].rearrange(
            "p (z i j) -> p z i j", z=2, i=GI) for i in range(3))
        LATE = ExitStack()
        o_t = sb("o_t", [P, 2, SEQ], at=LATE)
        o_n = sb("o_n", [P, 2, QB, P], at=LATE)
        LATE.close()

        ps = ctx.enter_context(nc.psum_tensor("ps", [P, 8, 512], F32))

        in_first = [sem(f"in_first{i}") for i in range(FIRST_MODS)]
        in_x, in_pos, in_vec, in_const, in_c = (sem(n) for n in (
            "in_x", "in_pos", "in_vec", "in_const", "in_c"))
        s5_in = Signal(sem("s5_in"), 16 * 4)
        mix_in = Signal(sem("mix_in"), 16 * 26)
        w_loaded = [sem(f"w_loaded{i}") for i in range(RING)]
        w_split_hi = Signal(sem("w_split_hi"), LAYER_CHUNKS)
        w_split_lo = Signal(sem("w_split_lo"), LAYER_CHUNKS, RING)
        w_used = Signal(sem("w_used"), LAYER_CHUNKS, RING)
        m_loaded = [sem(f"m_loaded{i}") for i in range(MOD_RING)]
        MODS = N_MOD * KT
        m_used = Signal(sem("m_used"), MODS, MOD_RING)
        acc_ready = Signal(sem("acc_ready"), N_MOD, 2)
        mod_psum = Signal(sem("mod_psum"), N_MOD, 2)
        mod_done = Signal(sem("mod_done"), N_MOD, 2)
        prologue = sem("prologue")
        prologue_d = sem("prologue_d")
        prologue_a = sem("prologue_a")
        credits = sem("credits")
        ms_ready = Signal(sem("ms_ready"), 4)
        rstd_ready = Signal(sem("rstd_ready"), 4)
        diag_ready = Signal(sem("diag_ready"), 4)
        bcast = Signal(sem("bcast"), 4)
        a_ready = Signal(sem("a_ready"), 3)
        ht_ready = Signal(sem("ht_ready"), 3 * KT)
        h_full = Signal(sem("h_full"), 3 * KT)
        h_hi_done = Signal(sem("h_hi_done"), 3 * KT)
        h_done = Signal(sem("h_done"), 3 * KT)
        silu_done = Signal(sem("silu_done"), 2 * FT)
        g_full = Signal(sem("g_full"), 2 * FT, 2)
        g_hi_done = Signal(sem("g_hi_done"), 2 * FT)
        g_done = Signal(sem("g_done"), 2 * FT, 2)
        x_new = Signal(sem("x_new"), 3 * KT, KT + 2)
        sq_done = Signal(sem("sq_done"), 3 * KT, KT)
        sq_sum = Signal(sem("sq_sum"), 3 * (KT - 1), KT - 1)
        ssq = Signal(sem("ssq"), 3, 1)
        z_copy = Signal(sem("z_copy"), 12)
        swap_mm = Signal(sem("swap_mm"), 8)
        rope_done = Signal(sem("rope_done"), 8)
        v_tr = Signal(sem("v_tr"), 1)
        v_done = Signal(sem("v_done"), 2)
        idx_mm = Signal(sem("idx_mm"), 12)
        idx_relu = Signal(sem("idx_relu"), 12)
        idx_acc = Signal(sem("idx_acc"), 12)
        mask_done = Signal(sem("mask_done"), QB)
        NA = QB * HEADS
        logit = Signal(sem("logit"), NA)
        masked = Signal(sem("masked"), NA)
        p_exp = Signal(sem("p_exp"), NA)
        pt_mm = Signal(sem("pt_mm"), NA)
        pt_copy = Signal(sem("pt_copy"), NA)
        pv = Signal(sem("pv"), NA)
        att_n = Signal(sem("att_n"), QB)
        att_sq = Signal(sem("att_sq"), QB)
        att_ms = Signal(sem("att_ms"), QB)
        att_rs = Signal(sem("att_rs"), QB)
        att_sc = Signal(sem("att_sc"), QB)
        att_tr = Signal(sem("att_tr"), QB)
        att_f = Signal(sem("att_f"), QB)
        att_hi = Signal(sem("att_hi"), QB)
        att_done = Signal(sem("att_done"), QB)
        s5_act = Signal(sem("s5_act"), 5)
        s5_sel = Signal(sem("s5_sel"), 1)
        s5_vec = Signal(sem("s5_vec"), 2)
        ct_mm = Signal(sem("ct_mm"), 1)
        ct_done = Signal(sem("ct_done"), 3)
        bb_done = Signal(sem("bb_done"), 1)
        toep0 = Signal(sem("toep0"), 1)
        prep = Signal(sem("prep"), 4 * 3)
        kk_mm = Signal(sem("kk_mm"), 4)
        kk_copy = Signal(sem("kk_copy"), 4 * 2)
        kk_d = Signal(sem("kk_d"), 4)
        toep_in = Signal(sem("toep_in"), 4 * 16 * L)
        w_tr = Signal(sem("w_tr"), 4)
        w_copy = Signal(sem("w_copy"), 4 * 2)
        un_tr = Signal(sem("un_tr"), 4)
        un_copy = Signal(sem("un_copy"), 4 * 2)
        u8_tr = Signal(sem("u8_tr"), 4)
        u8_copy = Signal(sem("u8_copy"), 4)
        st_mm = Signal(sem("st_mm"), 4)
        hs_done = Signal(sem("hs_done"), 4)
        y_mm = Signal(sem("y_mm"), 4)
        y_copy = Signal(sem("y_copy"), 4 * 2)
        y_tr = Signal(sem("y_tr"), 4)
        y_tile = Signal(sem("y_tile"), 4)
        y_act = Signal(sem("y_act"), 4 * 2)
        y_done = Signal(sem("y_done"), 4)
        glu_act = Signal(sem("glu_act"), ST)
        ssm_y = Signal(sem("ssm_y"), ST)
        ssm_sq = Signal(sem("ssm_sq"), ST)
        ssm_ss = Signal(sem("ssm_ss"), ST)
        ssm_f = Signal(sem("ssm_f"), ST)
        ssm_hi = Signal(sem("ssm_hi"), ST)
        mix_done = Signal(sem("mix_done"), ST)
        out_f = sem("out_f")
        out_tr = sem("out_tr")
        out_copy = sem("out_copy")
        out_dma = [sem(f"out_dma{i}") for i in range(2)]
        dve_step = sem("dve_step")
        pool_step = sem("pool_step")
        settled = sem("settled")

        w1 = [a["ffn1_w1"], a["ffn2_w1"]]
        w3 = [a["ffn1_w3"], a["ffn2_w3"]]
        w2 = [a["ffn1_w2"], a["ffn2_w2"]]

        def tiles(w, layer, k0, k, col, width=P):
            v = w.rearrange("l (k p) n -> l p k n", p=P)
            return v[ds(layer, 1), :, k0:k0 + k, ds(col, width)].rearrange("a p k n -> (a p) k n")

        def wait(eng, s, layer, k):
            eng.wait_ge(s.sem, s.after(layer, k))

        def settle(eng):
            eng.sem_inc(settled, 1)

        def used(eng, layer, c, shift=0):
            eng.wait_ge(w_used.sem, w_used.after(layer, c) + shift)

        def projected(eng, layer, e):
            n = e % KT
            used(eng, layer, MIX_BASE + 16 + n if e // KT == 1 else FFN_BASE[e // (2 * KT)] + 2 * FT + 3 * n + 2)

        def loads(c):
            return 2 if c % LAYER_CHUNKS in (MIX_BASE + 2, MIX_BASE + 3) else 1

        def slot_loaded(layer, c, turns):
            total = sum(loads(e) for e in range(c % RING, LAYER_CHUNKS, RING))
            upto = sum(loads(e) for e in range(c % RING, c + 1, RING))
            return 16 * total * layer + 16 * upto + 16 // RING * turns

        def down_chunk(j):
            return sum(DOWN_K[:j]), DOWN_K[j]

        def chunk_size(c):
            c %= LAYER_CHUNKS
            for b in FFN_BASE:
                if b + 2 * FT <= c < b + FFN_CHUNKS:
                    return DOWN_K[(c - b - 2 * FT) % 3] * P
            if MIX_BASE + 8 + ST <= c < MIX_BASE + 8 + 2 * ST:
                return ST * P
            return KT * P

        block = ctx.enter_context(nc.Block())

        @block.sync
        def _(sp):
            def load_w(layer, c, src, extra=0, shift=0):
                n = chunk_size(c)
                sp.wait_ge(w_split_lo.sem, w_split_lo.after(layer, c - RING) + shift)
                settle(sp)
                dst = stage[:, c % RING, 0:n]
                src = src if isinstance(src, tuple) else (src,)
                dst = dst.rearrange("p (k t n) -> p k t n", k=src[0].shape[1], t=len(src))
                for t, v in enumerate(src):
                    sp.dma_start(dst[:, :, t, :], v).then_inc(w_loaded[c % RING], 16)

            def load_mod(layer, q, src_layer, part, shift=0):
                sp.wait_ge(m_used.sem, m_used.after(layer, q - MOD_RING) + shift)
                src = a["mod_w"].rearrange("l k n -> (l k) n")[
                    ds(src_layer * D + (q % KT) * P, P), ds(part * D, D)]
                sp.dma_start(mod_stage[:, q % MOD_RING, :], src).then_inc(m_loaded[q % MOD_RING], 16)

            def load_up(layer, ffn, f, c, shift=0):
                load_w(layer, c, tiles(w1[ffn], layer, 0, KT, f * P), shift=shift)
                load_w(layer, c + 1, tiles(w3[ffn], layer, 0, KT, f * P), shift=shift)

            def mix_src(layer, m):
                w_in = a["w_in"]
                if m < 2:
                    return tiles(w_in, layer, 0, KT, COL_QI + m * P)
                if m in (2, 3):
                    col = COL_K if m == 2 else COL_K + HD
                    return tuple(tiles(w_in, layer, 0, KT, col + t * (COL_KI - COL_K), HD) for t in range(2))
                if m < 8:
                    return tiles(w_in, layer, 0, KT, (m - 4) * P)
                if m < 12:
                    return tiles(w_in, layer, 0, KT, COL_U + (m - 8) * P)
                if m < 16:
                    return tiles(a["glu_w"], layer, 0, ST, (m - 12) * P)
                return tiles(a["w_out"], layer, 0, KT, (m - 16) * P)

            def following(layer, ffn, m):
                if ffn == 0:
                    return mix_src(layer, m)
                return tiles((w1[0], w3[0])[m], (layer + 1) % DEPTH, 0, KT, 0)

            sp.dma_start(vraw[80:88, 0, :], a["c"].rearrange("o (k p) -> (o k) p", p=P)).then_inc(in_c, 16)
            sp.dma_start(ident[:], a["consts"][:, C_ID:C_ID + P]).then_inc(in_const, 16)
            sp.dma_start(cols[:], a["consts"][:, C_COLS:C_COLS + 4]).then_inc(in_const, 16)
            for l in range(DEPTH):
                sp.dma_start(vraw[0:72, 1 + l, :], a["mod_b"][l].rearrange("(k p) -> k p", p=P)).then_inc(in_vec, 16)
            sp.dma_start(x_in[:], a["x"].rearrange("o (b p) d -> p (o b) d", p=P)).then_inc(in_x, 16)
            for i in range(FIRST_MODS):
                part, k0, n = i * 2 // FIRST_MODS, i * 2 * KT // FIRST_MODS % KT, 2 * KT // FIRST_MODS
                src = a["mod_w"][0].rearrange("(k p) n -> p k n", p=P)[:, k0:k0 + n, part * D:(part + 1) * D]
                sp.dma_start(mod_first[:, part, k0:k0 + n, :], src).then_inc(in_first[i], 16)
            load_w(0, 0, tiles(w1[0], 0, 0, KT, 0))
            load_w(0, 1, tiles(w3[0], 0, 0, KT, 0))

            with sp.Fori(0, DEPTH) as l:
                for ffn in range(2):
                    c0 = FFN_BASE[ffn]
                    if ffn == 0:
                        for i, name in enumerate(("ssm_a_re", "ssm_a_im")):
                            sp.dma_start(s5_raw[:, i, :], a[name][ds(l, 1)].rearrange("o g p -> (o g) p")).then_inc(s5_in.sem, 16)
                        for g2 in range(2):
                            v = a["ssm_log_dt"][ds(l, 1)].rearrange("o (m t i) -> t o m i", t=2, i=GI)[g2]
                            sp.dma_start(s5_ldt[g2 * NS:(g2 + 1) * NS, :].rearrange("p (m i) -> p m i", i=GI),
                                         v.rearrange("o m i -> (o m) i").partition_broadcast(NS)).then_inc(s5_in.sem, 16)
                    if ffn == 1:
                        wait(sp, hs_done, l, 3)
                        settle(sp)
                    with sp.Fori(0, A_TURNS) as i:
                        for u in range(A_UNROLL):
                            load_up(l, ffn, A_UNROLL * i + (u + 1), c0 + 2 * (u + 1), shift=2 * A_UNROLL * i)
                            if ffn == 0:
                                for q in MOD_TURN[u]:
                                    load_mod(l, q, l, i + 2, shift=KT * i)
                    last = A_TURNS * A_UNROLL
                    q0 = A_TURNS * KT if ffn == 0 else (A_TURNS + 1) * KT
                    for f in (last, last + 1):
                        c = c0 + 2 * (f + 1)
                        if f == last:
                            load_up(l, ffn, f + 1, c)
                        else:
                            for j in range(2):
                                load_w(l, c + j, tiles(w2[ffn], l, *down_chunk(j), 0))
                        for q in MOD_REST[f - last]:
                            load_mod(l, q0 + q, l, 7 + ffn)
                    b0 = c0 + 2 * FT
                    for n in range(KT):
                        for e in range(3 * n + AHEAD, 3 * n + AHEAD + 3):
                            if e < 3 * KT:
                                load_w(l, b0 + e, tiles(w2[ffn], l, *down_chunk(e % 3), (e // 3) * P))
                            else:
                                load_w(l, b0 + e, following(l, ffn, e - 3 * KT))
                        if ffn == 1:
                            for q in (2 * n, 2 * n + 1):
                                load_mod(l, q0 + KT + q, (l + 1) % DEPTH, q // KT)
                    if ffn == 0:
                        for m in range(AHEAD, MIX_FIRST):
                            load_w(l, MIX_BASE + m, mix_src(l, m))
                        projected(sp, l, KT - 1)
                        for i in range(5):
                            sp.dma_start(swaps[:, i, :], a["consts"][:, (i + 1) * P:(i + 2) * P]).then_inc(mix_in.sem, 16)
                        for i, name in enumerate(("ssm_c_re", "ssm_c_im")):
                            v = a[name][ds(l, 1)].rearrange("o (m t i) c p -> o (i c) m t p", t=2, i=GI)
                            v = v.rearrange("o q m t p -> (o q) m t p")
                            for g2 in range(2):
                                sp.dma_start(c_raw[:, i, :, g2 * NS:(g2 + 1) * NS], v[:, :, g2, :]).then_inc(mix_in.sem, 16)
                        for i, name in enumerate(("ssm_b_re", "ssm_b_im")):
                            for g2 in range(2):
                                v = a[name][ds(l, 1)].rearrange("o (m t i) p c -> m t o p i c", t=2, i=GI)
                                for m in range(4):
                                    sp.dma_start(b_raw[g2 * NS:(g2 + 1) * NS, i, m, :].rearrange("p (i c) -> p i c", i=GI),
                                                 v[m, g2].rearrange("o p i c -> (o p) i c")).then_inc(mix_in.sem, 16)
                        sp.dma_start(d_raw[:], a["ssm_d"][ds(l, 1)].rearrange("o g c -> c (o g)"), allow_slow_non_contiguous=True).then_inc(mix_in.sem, 16)
                        for m in range(MIX_FIRST, MIX_CHUNKS + AHEAD):
                            if m < MIX_CHUNKS:
                                load_w(l, MIX_BASE + m, mix_src(l, m))
                            else:
                                w = (w1[1], w3[1])[m - MIX_CHUNKS]
                                load_w(l, MIX_BASE + m, tiles(w, l, 0, KT, 0))

        @block.scalar
        def _(act):
            def split_hi(layer, c, shift=0):
                n, turns = chunk_size(c), shift
                act.wait_ge(w_loaded[c % RING], slot_loaded(layer, c, turns))
                act.wait_ge(w_used.sem, w_used.after(layer, c - RING) + turns)
                nc.scalar.activation(w_hi[:, c % RING, 0:n], stage[:, c % RING, 0:n], ACT.Copy).then_inc(w_split_hi.sem, 1)

            def squares(layer, k):
                n = k % KT
                wait(act, x_new, layer, k)
                if n >= 3:
                    wait(act, sq_sum, layer, k // KT * (KT - 1) + n - 3)
                dst = tmp_b[:, n % 2, :] if n else tmp_a[:, 0, :]
                nc.scalar.activation(dst, x[:, n, :], ACT.Square).then_inc(sq_done.sem, 1)

            def norm_hi(layer, k3, shift_part):
                wait(act, a_ready, layer, k3)
                wait(act, bcast, layer, (0, 1, 3)[k3])
                for k in range(KT):
                    e = k3 * KT + k
                    wait(act, ht_ready, layer, e)
                    if k >= 2:
                        wait(act, h_done, layer, e - 2)
                    nc.scalar.activation(tmp_b[:, k % 2, :], tmp_a[:, k % 2, :], ACT.Identity, scale=a_col[:, k:k + 1],
                                         bias=modc[:, shift_part, k:k + 1]).then_inc(h_full.sem, 1)
                    wait(act, h_full, layer, e)
                    nc.scalar.activation(h_hi[:, k, :], tmp_b[:, k % 2, :], ACT.Copy).then_inc(h_hi_done.sem, 1)

            act.dma_start(vraw[0:48, 0, :], a["norm_g"].rearrange("l t (k p) -> (l t k) p", p=P)).then_inc(in_c, 16)
            act.dma_start(vraw[48:56, 0, :], a["final_g"].rearrange("(k p) -> k p", p=P)).then_inc(in_c, 16)
            act.dma_start(vraw[56:64, 0, :], a["attn_gain"].rearrange("l (k p) -> (l k) p", p=P)).then_inc(in_c, 16)
            act.dma_start(vraw[64:72, 0, :], a["ssm_gain"].rearrange("l (k p) -> (l k) p", p=P)).then_inc(in_c, 16)
            act.dma_start(vraw[72:80, 0, :], a["glu_b"].rearrange("l (k p) -> (l k) p", p=P)).then_inc(in_c, 16)
            act.dma_start(pos_i[:], a["positions"].partition_broadcast(P).rearrange("p o t -> p (o t)")).then_inc(in_pos, 16)
            act.wait_ge(credits, 6)
            nc.scalar.activation(c_silu[:], vcols[:, 80:88], ACT.Silu).then_inc(prologue_a, 1)
            act.wait_ge(prologue_d, 1)
            nc.scalar.activation(rope_s[:], tmp_a[:, 0, :], ACT.Sin).then_inc(prologue_a, 1)
            nc.scalar.activation(rope_c[:], tmp_a[:, 1, :], ACT.Sin).then_inc(prologue_a, 1)
            for k in range(KT):
                squares(0, k - KT)
            for c in range(AHEAD):
                split_hi(0, c)

            def s5_parameters(l):
                wait(act, s5_sel, l, 0)
                nc.scalar.activation(s5_a[:].rearrange("p t q -> p (t q)"), ps[:, 6, 16:16 + 2 * NQ], ACT.Copy).then_inc(s5_act.sem, 1)
                act.wait_ge(s5_in.sem, 64 * l + 64)
                nc.scalar.activation(s5_t[:, 0, :], s5_ldt[:], ACT.Exp).then_inc(s5_act.sem, 1)

            def s5_exp_sin(l):
                wait(act, s5_vec, l, 0)
                nc.scalar.activation(s5_t[:, 3, :], s5_t[:, 1, :], ACT.Exp).then_inc(s5_act.sem, 1)
                nc.scalar.activation(mag_l[:], s5_t[:, 1, :], ACT.Exp, scale=float(L)).then_inc(s5_act.sem, 1)
                wait(act, s5_vec, l, 1)
                nc.scalar.activation(s5_t[:, 6:8, :].rearrange("p t q -> p (t q)"),
                                     s5_t[:, 4:6, :].rearrange("p t q -> p (t q)"), ACT.Sin).then_inc(s5_act.sem, 1)

            def ffn_act(l, ffn):
                c0, f0 = FFN_BASE[ffn], ffn * FT

                def tile(f, parity, shift):
                    used(act, l, c0 + 2 * f + 1, 2 * shift)
                    nc.scalar.activation(tmp_a[:, parity, :], ps[:, 2 * parity, :], ACT.Silu).then_inc(silu_done.sem, 1)
                    act.wait_ge(g_full.sem, g_full.after(l, f0 + f) + shift)
                    nc.scalar.activation(g_hi[:, ds(f + shift, 1), :].rearrange("p a n -> p (a n)") if not isinstance(shift, int) else g_hi[:, f, :],
                                         tmp_b[:, parity, :], ACT.Copy).then_inc(g_hi_done.sem, 1)

                with act.Fori(0, A_TURNS) as i:
                    for u in range(A_UNROLL):
                        for j in range(2):
                            split_hi(l, c0 + 2 * (u + 1) + j, shift=2 * A_UNROLL * i)
                        tile(u, u % 2, A_UNROLL * i)
                for f in (FT - 2, FT - 1):
                    for j in range(2):
                        split_hi(l, c0 + 2 * (f + 1) + j)
                    tile(f, f % 2, 0)
                for n in range(KT):
                    for e in range(3 * n + AHEAD, 3 * n + AHEAD + 3):
                        split_hi(l, c0 + 2 * FT + e)
                    if ffn == 0 and n == 0:
                        s5_parameters(l)
                    if ffn == 0 and n == 2:
                        s5_exp_sin(l)
                    squares(l, 2 * KT * ffn + n)

            def mixer_act(l):
                m0 = MIX_BASE

                def z_tile(t):
                    used(act, l, m0 + t)
                    if t < 8:
                        if t in (2, 3):
                            wait(act, rope_done, l, t - 2)
                        elif t == 4:
                            wait(act, rope_done, l, 3)
                        elif t == 5:
                            wait(act, v_tr, l, 0)
                        elif t > 5:
                            wait(act, rope_done, l, t - 2)
                        nc.scalar.activation(z_t[:, t % 2, :], ps[:, t % 2, :], ACT.Copy).then_inc(z_copy.sem, 1)
                    else:
                        nc.scalar.activation(u_t[:, t - 8, :, :], ps[:, t % 2, :].rearrange("p (j s) -> p s j", s=L),
                                             ACT.Copy).then_inc(z_copy.sem, 1)

                def index_relu(n):
                    b = n // IDX_HEADS + 1
                    wait(act, idx_mm, l, n)
                    if n >= 2:
                        wait(act, idx_acc, l, n - 2)
                    w = (b + 1) * P
                    nc.scalar.activation(tmp_a[:, n % 2, 0:w], ps[:, 4 + n % 2, 0:w], ACT.Relu).then_inc(idx_relu.sem, 1)

                def v_copy():
                    wait(act, v_tr, l, 0)
                    v = ps[:, 4, :].rearrange("p (b n) -> p b n", b=QB)
                    nc.scalar.activation(v_n[:], v[:, :, 0:HD], ACT.Copy).then_inc(v_done.sem, 1)
                    nc.scalar.activation(wi_n[:], v[:, :, HD:HD + IDX_HEADS], ACT.Copy, scale=IDX_SCALE).then_inc(v_done.sem, 1)

                def ct_copy():
                    wait(act, ct_mm, l, 0)
                    v = ps[:, 7, :].rearrange("p (t n) -> p t n", t=2)
                    for i, (src, scale) in enumerate(((0, 1.0), (1, 1.0), (0, -1.0))):
                        nc.scalar.activation(ct[:, i, :, :].rearrange("p m q -> p (m q)"), v[:, src, :], ACT.Copy,
                                             scale=scale).then_inc(ct_done.sem, 1)

                def p_exps(e):
                    b, h = e // HEADS, e % HEADS
                    w = (b + 1) * P
                    wait(act, masked, l, e)
                    if e >= 2:
                        wait(act, pt_mm, l, e - 2)
                    nc.scalar.activation(tmp_b[:, e % 2, 0:w], tmp_a[:, e % 2, 0:w], ACT.Exp, scale=-1.0,
                                         bias=nmax[:, e % 2:e % 2 + 1], accum_out=rsum[:, b % 2, h:h + 1]).then_inc(p_exp.sem, 1)

                def p_copy(e):
                    w = (e // HEADS + 1) * P
                    wait(act, pt_mm, l, e)
                    if e >= 2:
                        wait(act, pv, l, e - 2)
                    nc.scalar.activation(pt[:, e % 2, 0:w], ps[:, 2, 0:w], ACT.Copy).then_inc(pt_copy.sem, 1)

                def att_square(b):
                    wait(act, att_n, l, b)
                    if b:
                        wait(act, att_hi, l, b - 1)
                    nc.scalar.activation(z_t[:, 0, :], att[:].rearrange("p h d -> p (h d)"), ACT.Square,
                                         accum_out=att_ss[:, 0:1]).then_inc(att_sq.sem, 1)

                def att_high(b):
                    wait(act, att_f, l, b)
                    nc.scalar.activation(h_hi[:, 0:AT, b * P:(b + 1) * P], z_t[:, 1, :].rearrange("p (m t) -> p m t", m=AT),
                                         ACT.Copy).then_inc(att_hi.sem, 1)

                def half(i):
                    return slice(i * 512, (i + 1) * 512)

                def s5_kk(m):
                    wait(act, kk_mm, l, m)
                    for i in range(2):
                        nc.scalar.activation(kk_y[0:GC, half(i)], ps[0:GC, 4 + i, :], ACT.Copy).then_inc(kk_copy.sem, 1)

                def s5_toeplitz(m):
                    wait(act, kk_d, l, m)
                    wait(act, toep0, l, 0)
                    kk = kk_y[0:GC, :].rearrange("c (g n) -> c g n", g=2 * GI)
                    for s in range(L):
                        act.dma_start(toep[s * GC:(s + 1) * GC, :, s * GC:P], kk[:, :, 0:P - s * GC]).then_inc(toep_in.sem, 16)

                def s5_w(m):
                    wait(act, w_tr, l, m)
                    for i in range(2):
                        nc.scalar.activation(wst[:, i, :, :].rearrange("p i n -> p (i n)"), ps[:, 4 + i, :], ACT.Copy).then_inc(w_copy.sem, 1)

                def s5_un(m):
                    wait(act, un_tr, l, m)
                    for i in range(2):
                        nc.scalar.activation(un[:, :, 4 * i:4 * i + 4, :].rearrange("j g s c -> j s g c"),
                                             ps[0:J, 4 + i, :].rearrange("j (s g c) -> j s g c", s=4, c=GC),
                                             ACT.Copy).then_inc(un_copy.sem, 1)

                def s5_u8(m):
                    wait(act, u8_tr, l, m)
                    nc.scalar.activation(u8[:].rearrange("p g j -> p (g j)"), ps[:, 4, :], ACT.Copy).then_inc(u8_copy.sem, 1)

                def s5_y(m):
                    wait(act, y_mm, l, m)
                    act.wait_ge(toep_in.sem, toep_in.per * l + 16 * L * (m + 1))
                    for i in range(2):
                        nc.scalar.activation(kk_y[:].rearrange("j (t g c) -> j g t c", t=L, c=GC)[:, 4 * i:4 * i + 4],
                                             ps[0:J, 4 + i, :].rearrange("j (g t c) -> j g t c", g=4, c=GC),
                                             ACT.Copy).then_inc(y_copy.sem, 1)

                def s5_y_tile(m):
                    wait(act, y_tr, l, m)
                    nc.scalar.activation(u_t[:, m].rearrange("p a b -> p (a b)").rearrange("p (j t) -> p j t", t=L),
                                         ps[:, 6, :].rearrange("p (t j) -> p j t", t=L), ACT.Copy).then_inc(y_tile.sem, 1)

                def gelu(m):
                    y = u_t[:, m].rearrange("p a b -> p (a b)")
                    nc.scalar.activation(y, y, ACT.Gelu_apprx_tanh).then_inc(y_act.sem, 1)
                    wait(act, y_act, l, 2 * m)
                    nc.scalar.activation(h_hi[:, AT + m, :], y, ACT.Copy).then_inc(y_act.sem, 1)

                def s5_step(e):
                    m, h = divmod(e + S5_LEAD, HEADS)
                    if h == 0 and m:
                        s5_y_tile(m - 1)
                    if m < 4 and h in (1, 2, 3, 4, 7):
                        if h == 2:
                            s5_toeplitz(m)
                        {1: s5_kk, 2: s5_w, 3: s5_un, 4: s5_u8, 7: s5_y}[h](m)

                norm_hi(l, 1, 3)
                for t in range(12):
                    split_hi(l, m0 + t + AHEAD)
                    z_tile(t)
                    if t == 2:
                        ct_copy()
                    if t == 4:
                        v_copy()
                    if t in (6, 7, 8):
                        for n in range(IDX_HEADS):
                            index_relu((t - 6) * IDX_HEADS + n)
                    if t > 12 - S5_LEAD:
                        s5_step(t - 12)
                for n in range(2):
                    split_hi(l, m0 + 12 + n + AHEAD)
                wait(act, h_done, l, 2 * KT - 1)
                for b in range(QB):
                    for h in range(HEADS):
                        p_exps(b * HEADS + h)
                        s5_step(b * HEADS + h)
                        p_copy(b * HEADS + h)
                        if b and h == 2:
                            att_square(b - 1)
                        if b and h == 7:
                            att_high(b - 1)
                att_square(QB - 1)
                wait(act, y_tile, l, ST - 1)
                for m in range(ST):
                    gelu(m)
                for n in range(ST):
                    used(act, l, m0 + 12 + n)
                    if n >= 2:
                        wait(act, ssm_y, l, n - 2)
                    nc.scalar.activation(tmp_a[:, n % 2, :], ps[:, n, :], ACT.Tanh, scale=0.5,
                                         bias=half_bias[:, n:n + 1]).then_inc(glu_act.sem, 1)
                    if n < 2:
                        split_hi(l, m0 + 14 + n + AHEAD)
                    wait(act, ssm_y, l, n)
                    if n >= 2:
                        wait(act, ssm_ss, l, n - 2)
                    nc.scalar.activation(tmp_b[:, n % 2, :], q_t[:, n, :], ACT.Square).then_inc(ssm_sq.sem, 1)
                att_high(QB - 1)
                for n in range(ST):
                    wait(act, ssm_f, l, n)
                    nc.scalar.activation(h_hi[:, AT + n, :], tmp_a[:, n % 2, :], ACT.Copy).then_inc(ssm_hi.sem, 1)
                for n in range(KT):
                    split_hi(l, m0 + 16 + n + AHEAD)
                    squares(l, KT + n)

            with act.Fori(0, DEPTH) as l:
                norm_hi(l, 0, 0)
                ffn_act(l, 0)
                mixer_act(l)
                norm_hi(l, 2, 6)
                ffn_act(l, 1)

            for n in range(KT):
                act.wait_ge(out_tr, n + 1)
                if n >= 2:
                    act.wait_ge(out_dma[n % 2], 16 * (n // 2))
                nc.scalar.activation(o_n[:, n % 2, :, :].rearrange("p b f -> p (b f)"), ps[:, 4 + n % 2, :], ACT.Copy).then_inc(out_copy, 1)
                act.wait_ge(out_copy, n + 1)
                act.dma_start(a["out"].rearrange("o (b p) d -> p (o b) d", p=P)[:, :, n * P:(n + 1) * P],
                              o_n[:, n % 2, :, :]).then_inc(out_dma[n % 2], 16)
            for i in range(2):
                act.wait_ge(out_dma[i], 16 * KT // 2)

        @block.vector
        def _(dve):
            V = nc.vector

            def split_lo(layer, c, shift=0):
                n = chunk_size(c)
                dve.wait_ge(w_split_hi.sem, w_split_hi.after(layer, c) + shift)
                V.tensor_tensor(w_lo[:, c % RING, 0:n], stage[:, c % RING, 0:n],
                                w_hi[:, c % RING, 0:n].bitcast(F32), ALU.subtract).then_inc(w_split_lo.sem, 1)

            def mod_chunk(layer, q, shift=0, turn=0):
                s, turns = q % MOD_RING, shift
                per = MODS // MOD_RING
                chunk = mod_stage[:, s, :]
                dve.wait_ge(m_loaded[s], 16 * (layer * per + q // MOD_RING + 1) + 16 // MOD_RING * turns)
                dve.wait_ge(m_used.sem, m_used.after(layer, q - 1) + turns)
                if q % KT == 0:
                    dve.wait_ge(mod_psum.sem, mod_psum.after(layer, q // KT - 1) + turn)
                k = q % KT
                if k == 0:
                    i = V.tensor_scalar(mod_acc[:], chunk, c_silu[:, k:k + 1], None, ALU.mult)
                else:
                    i = V.scalar_tensor_tensor(out=mod_acc[:], in0=chunk, scalar=c_silu[:, k:k + 1],
                                               in1=mod_acc[:], op0=ALU.mult, op1=ALU.add)
                i.then_inc(m_used.sem, 1)

            def mod_out(layer, j, part, bias_layer, turn=0):
                dve.wait_ge(mod_psum.sem, mod_psum.after(layer, j) + turn)
                V.tensor_tensor(modc[:, ds(part, 1), :].rearrange("p a k -> p (a k)") if not isinstance(part, int) else modc[:, part, :],
                                ps[:, 7, 0:KT], modb[:, ds(bias_layer * (N_MOD * KT) + part * KT, KT)],
                                ALU.add).then_inc(mod_done.sem, 1)

            def rms(layer, idx, width, step):
                V.tensor_scalar(ms[:], ps[:, 6, 0:QB], 1.0 / width, EPS, ALU.mult, ALU.add).then_inc(ms_ready.sem, 1)
                wait(dve, rstd_ready, layer, idx)
                V.tensor_tensor(tmp_b[:, 0, :].rearrange("p (b t) -> p b t", b=QB),
                                ident[:].unsqueeze(1).broadcast_to((P, QB, P)),
                                rstd[:].unsqueeze(2).broadcast_to((P, QB, P)), ALU.mult).then_inc(diag_ready.sem, 1)

            def norm(layer, k3, idx, scale_part, shift_part, gate_part, gate_scale, step):
                wait(dve, ssq, layer, k3 - 1)
                rms(layer, idx, D, step)
                wait(dve, mod_done, layer, scale_part - 2)
                V.scalar_tensor_tensor(out=a_col[:], in0=modc[:, scale_part, :], scalar=1.0,
                                       in1=vcols[:, ds(layer * (3 * KT) + k3 * KT, KT)],
                                       op0=ALU.add, op1=ALU.mult).then_inc(a_ready.sem, 1)
                wait(dve, bcast, layer, idx)

                def full_lo(k):
                    e = k3 * KT + k
                    wait(dve, h_hi_done, layer, e)
                    V.tensor_tensor(h_lo[:, k, :], tmp_b[:, k % 2, :], h_hi[:, k, :].bitcast(F32),
                                    ALU.subtract).then_inc(h_done.sem, 1)

                for k in range(KT + 2):
                    if k < KT:
                        e = k3 * KT + k
                        if k == 0:
                            wait(dve, a_ready, layer, k3)
                        if k >= 2:
                            wait(dve, h_full, layer, e - 2)
                        V.tensor_tensor(tmp_a[:, k % 2, :], x[:, k, :], ps[:, 7, :], ALU.mult).then_inc(ht_ready.sem, 1)
                    if k >= 2:
                        full_lo(k - 2)

            def add_squares(layer, k):
                n = k % KT
                if n == 0:
                    return
                e = k // KT * (KT - 1) + n - 1
                wait(dve, sq_done, layer, k)
                if n > 1:
                    wait(dve, sq_sum, layer, e - 1)
                V.tensor_tensor(tmp_a[:, 0, :], tmp_a[:, 0, :], tmp_b[:, n % 2, :], ALU.add).then_inc(sq_sum.sem, 1)

            def gates(layer, k3, gate_part, gate_scale):
                wait(dve, mod_done, layer, gate_part - 2)
                return V.tensor_scalar(gate[:, k3, :], modc[:, gate_part, :], gate_scale, None, ALU.mult)

            def update(layer, k3, n):
                e = k3 * KT + n
                projected(dve, layer, e)
                V.scalar_tensor_tensor(out=x[:, n, :], in0=ps[:, 4 + n % 2, :], scalar=gate[:, k3, n:n + 1],
                                       in1=x[:, n, :], op0=ALU.mult, op1=ALU.add).then_inc(x_new.sem, 1)

            def reduce_angle(step, z, n, r):
                step(V.tensor_scalar(n, z, INV_2PI, ROUND, ALU.mult, ALU.add))
                step(V.tensor_scalar(n, n, ROUND, None, ALU.subtract))
                step(V.scalar_tensor_tensor(out=r, in0=n, scalar=-TWO_PI_A, in1=z, op0=ALU.mult, op1=ALU.add))
                step(V.scalar_tensor_tensor(out=r, in0=n, scalar=-TWO_PI_B, in1=r, op0=ALU.mult, op1=ALU.add))
                step(V.scalar_tensor_tensor(out=r, in0=n, scalar=-TWO_PI_C, in1=r, op0=ALU.mult, op1=ALU.add))
                step(V.tensor_scalar(r, r, float(np.float32(np.pi)) - 3e-7, -float(np.float32(np.pi)) + 3e-7, ALU.min, ALU.max))

            def cos_angle(step, r, c):
                step(V.tensor_scalar(c, r, -1.0, None, ALU.mult))
                step(V.tensor_tensor(c, c, r, ALU.max))
                step(V.tensor_scalar(c, c, -1.0, HALF_PI, ALU.mult, ALU.add))

            first = Chain(dve, credits, 0, 0)
            first(V.memset(ones[:], 1.0), V.memset(mhalf[:], -0.5))
            V.memset(ms[:, 0:1], 0.0).then_inc(w_split_lo.sem, RING)
            V.memset(ms[:, 1:2], 0.0).then_inc(w_used.sem, RING)
            V.memset(ms[:, 2:3], 0.0).then_inc(m_used.sem, MOD_RING)
            V.memset(ms[:, 3:4], 0.0).then_inc(g_full.sem, 2)
            V.memset(rstd[:, 3:4], 0.0).then_inc(g_done.sem, 2)
            V.memset(rstd[:, 0:1], 0.0).then_inc(x_new.sem, 2)
            first(V.memset(rstd[:, 2:3], 0.0))
            dve.wait_ge(prologue, 3)
            first(V.tensor_copy(vcols[:], ps[:, 4, 0:88]), V.tensor_copy(modb[:, 0:72], ps[:, 5, 0:72]),
                  V.tensor_copy(modb[:, 72:144], ps[:, 5, 128:200]))
            dve.wait_ge(in_pos, 16)
            dve.wait_ge(in_const, 32)
            ang, cnt = tmp_b[:, 0, :], tmp_b[:, 1, :]
            first(V.tensor_copy(ang, pos_i[:]))
            first(V.tensor_scalar(ang, ang, cols[:, 0:1], None, ALU.mult))
            reduce_angle(first, ang, cnt, tmp_a[:, 0, :])
            cos_angle(first, tmp_a[:, 0, :], tmp_a[:, 1, :])
            V.memset(s5_t[:, 0, 0:1], 0.0).then_inc(prologue_d, 1)
            dve.wait_ge(prologue_a, 3)
            first(V.tensor_scalar(rope_s[:], rope_s[:], cols[:, 1:2], None, ALU.mult),
                  V.tensor_scalar(rope_c[:], rope_c[:], cols[:, 2:3], cols[:, 3:4], ALU.mult, ALU.add))
            def first_chunk(part, k):
                acc = (mod_acc, mod_acc_b)[part]
                dve.wait_ge(in_first[(part * KT + k) * FIRST_MODS // (2 * KT)], 16)
                if k == 0:
                    first(V.tensor_scalar(acc[:], mod_first[:, part, k, :], c_silu[:, k:k + 1], None, ALU.mult))
                else:
                    first(V.scalar_tensor_tensor(out=acc[:], in0=mod_first[:, part, k, :], scalar=c_silu[:, k:k + 1],
                                                 in1=acc[:], op0=ALU.mult, op1=ALU.add))
                if k == KT - 1:
                    V.memset(s5_t[:, 1, part:part + 1], 0.0).then_inc(acc_ready.sem, 1)

            for n in range(KT):
                dve.wait_ge(prologue, 4 + n)
                V.tensor_copy(x[:, n, :], ps[:, 4 + n % 2, :]).then_inc(x_new.sem, 1)
                if n:
                    add_squares(0, n - 1 - KT)
                if n:
                    first_chunk(0, n - 1)
            first_chunk(0, KT - 1)
            add_squares(0, -1)
            for k in range(KT):
                first_chunk(1, k)
                if k == KT // 2:
                    mod_out(0, -2, 0, 0)
            for c in range(AHEAD):
                split_lo(0, c)
            mod_out(0, -1, 1, 0)

            def acc_done(layer, q, slot, shift=0):
                dve.wait_ge(m_used.sem, m_used.after(layer, q) + shift)
                V.memset(s5_t[:, 13, slot:slot + 1], 0.0).then_inc(acc_ready.sem, 1)

            def cmul(step, o, p, q, t):
                step(V.tensor_tensor(o[0], p[0], q[0], ALU.mult), V.tensor_tensor(t, p[1], q[1], ALU.mult))
                step(V.tensor_tensor(o[0], o[0], t, ALU.subtract), V.tensor_tensor(o[1], p[0], q[1], ALU.mult))
                step(V.tensor_tensor(t, p[1], q[0], ALU.mult))
                step(V.tensor_tensor(o[1], o[1], t, ALU.add))

            T = lambda i: s5_t[:, i, :]
            ar, ai = s5_a[:, 0, :], s5_a[:, 1, :]
            mag, sn, cs = T(3), T(6), T(7)

            def s5_angles(l, step):
                wait(dve, s5_act, l, 1)
                step(V.tensor_tensor(T(2), ai, T(0), ALU.mult))
                V.tensor_tensor(T(1), ar, T(0), ALU.mult).then_inc(s5_vec.sem, 1)
                reduce_angle(step, T(2), T(8), T(4))
                cos_angle(step, T(4), T(5))
                V.memset(T(9)[:, 0:1], 0.0).then_inc(s5_vec.sem, 1)

            def s5_powers(l, step):
                wait(dve, s5_act, l, 4)
                one = (pw[:, 0, 0, :], pw[:, 1, 0, :])
                step(V.memset(one[0], 1.0), V.memset(one[1], 0.0),
                     V.tensor_tensor(pw[:, 0, 1, :], mag, cs, ALU.mult),
                     V.tensor_tensor(pw[:, 1, 1, :], mag, sn, ALU.mult))
                step_p = 1
                t4 = s5_t[:, 8:12, :]
                while step_p < L:
                    top = [pw[:, z, step_p:step_p + 1, :].broadcast_to((P, step_p, NQ)) for z in range(2)]
                    cmul(step, [pw[:, z, step_p + 1:2 * step_p + 1, :] for z in range(2)],
                         [pw[:, z, 1:step_p + 1, :] for z in range(2)], top, t4[:, 0:step_p, :])
                    step_p *= 2

            def s5_rotations(l, step):
                cur = (cs, sn)
                spare = [(T(8), T(9)), (T(10), T(11))]
                for k in range(3 + 5):
                    nxt = (en[:, 0, k - 2, :], en[:, 1, k - 2, :]) if k >= 2 else spare[k % 2]
                    step(V.tensor_tensor(nxt[0], cur[0], cur[0], ALU.mult), V.tensor_tensor(T(12), cur[1], cur[1], ALU.mult),
                         V.scalar_tensor_tensor(out=nxt[1], in0=cur[0], scalar=2.0, in1=cur[1], op0=ALU.mult, op1=ALU.mult))
                    step(V.tensor_tensor(nxt[0], nxt[0], T(12), ALU.subtract))
                    cur = nxt

            def s5_factor(l, step):
                step(V.tensor_tensor(T(8), ar, ar, ALU.mult), V.tensor_tensor(T(9), ai, ai, ALU.mult),
                     V.tensor_scalar(T(10), pw[:, 0, 1, :], 1.0, None, ALU.subtract))
                step(V.tensor_tensor(T(8), T(8), T(9), ALU.add))
                step(V.reciprocal(T(8), T(8)))
                nr, ni = T(10), pw[:, 1, 1, :]
                step(V.tensor_tensor(T(9), nr, ar, ALU.mult), V.tensor_tensor(T(11), ni, ai, ALU.mult),
                     V.tensor_tensor(T(12), nr, ai, ALU.mult))
                step(V.tensor_tensor(T(9), T(9), T(11), ALU.add), V.tensor_tensor(T(7), ni, ar, ALU.mult))
                step(V.tensor_tensor(T(7), T(7), T(12), ALU.subtract))
                step(V.tensor_tensor(fz[:, 0, :], T(9), T(8), ALU.mult), V.tensor_tensor(fz[:, 1, :], T(7), T(8), ALU.mult))

            def ffn_dve(l, ffn):
                c0, f0 = FFN_BASE[ffn], ffn * FT
                q0 = A_TURNS * KT if ffn == 0 else (A_TURNS + 1) * KT

                def product(f, parity, shift):
                    dve.wait_ge(silu_done.sem, silu_done.after(l, f0 + f) + shift)
                    dve.wait_ge(g_done.sem, g_done.after(l, f0 + f - 2) + shift)
                    V.tensor_tensor(tmp_b[:, parity, :], tmp_a[:, parity, :], ps[:, 2 * parity + 1, :], ALU.mult).then_inc(g_full.sem, 1)

                def product_lo(f, parity, shift):
                    dve.wait_ge(g_hi_done.sem, g_hi_done.after(l, f0 + f) + shift)
                    static = isinstance(shift, int)
                    hi = g_hi[:, f, :] if static else g_hi[:, ds(f + shift, 1), :].rearrange("p a n -> p (a n)")
                    lo = g_lo[:, f, :] if static else g_lo[:, ds(f + shift, 1), :].rearrange("p a n -> p (a n)")
                    V.tensor_tensor(lo, tmp_b[:, parity, :], hi.bitcast(F32), ALU.subtract).then_inc(g_done.sem, 1)

                settle(dve)
                with dve.Fori(0, A_TURNS) as i:
                    for u in range(A_UNROLL):
                        for j in range(2):
                            split_lo(l, c0 + 2 * (u + 1) + j, shift=2 * A_UNROLL * i)
                        if ffn == 0:
                            for q in MOD_TURN[u]:
                                mod_chunk(l, q, shift=KT * i, turn=i)
                                if q == KT - 1:
                                    acc_done(l, KT - 1, 0, shift=KT * i)
                        product(u, u % 2, A_UNROLL * i)
                        product_lo(u, u % 2, A_UNROLL * i)
                    if ffn == 0:
                        mod_out(l, 0, i + 2, l, turn=i)
                for f in (FT - 2, FT - 1):
                    for j in range(2):
                        split_lo(l, c0 + 2 * (f + 1) + j)
                    for q in MOD_REST[f - FT + 2]:
                        mod_chunk(l, q0 + q)
                        if q == KT - 1:
                            acc_done(l, q0 + q, 1)
                    product(f, f % 2, 0)
                    product_lo(f, f % 2, 0)
                mod_out(l, q0 // KT, 7 + ffn, l)
                step = Chain(dve, dve_step, l, DVE_STEPS)
                step.n = steps[0]
                step(gates(l, 2 * ffn, 8 if ffn else 2, 0.5))
                for n in range(KT):
                    for e in range(3 * n + AHEAD, 3 * n + AHEAD + 3):
                        split_lo(l, c0 + 2 * FT + e)
                    if ffn == 1:
                        for q in (2 * n, 2 * n + 1):
                            mod_chunk(l, q0 + KT + q)
                        if n % 4 == 3:
                            acc_done(l, q0 + KT + 2 * n + 1, 2)
                    if n:
                        add_squares(l, 2 * ffn * KT + n - 1)
                    update(l, 2 * ffn, n)
                    if ffn == 0 and 1 <= n <= 4:
                        (s5_angles, s5_powers, s5_rotations, s5_factor)[n - 1](l, step)
                    if ffn == 1 and n % 4 == 3:
                        mod_out(l, q0 // KT + 1 + n // 4, n // 4, (l + 1) % DEPTH)
                add_squares(l, 2 * ffn * KT + KT - 1)
                steps[0] = step.n

            def mixer_dve(l, step):
                m0 = MIX_BASE

                def rope(r):
                    dst = (qi_t[:, 0, :], qi_t[:, 1, :], ki_t[:], k_t[:], *(q_t[:, i, :] for i in range(AT)))[r]
                    wait(dve, swap_mm, l, r)
                    src = ps[:, 2, :] if r in (2, 3) else z_t[:, r % 2, :]
                    step(V.tensor_tensor(tmp_b[:, 0, :], src, rope_c[:], ALU.mult),
                         V.tensor_tensor(tmp_b[:, 1, :], ps[:, 3, :], rope_s[:], ALU.mult))
                    V.tensor_tensor(dst, tmp_b[:, 0, :], tmp_b[:, 1, :], ALU.add).then_inc(rope_done.sem, 1)
                    wait(dve, rope_done, l, r)

                def b_bar():
                    dve.wait_ge(mix_in.sem, mix_in.per * (l + 1))
                    f = [fz[:, z, :].rearrange("p (m i) -> p m i", i=GI).unsqueeze(3).broadcast_to((P, 4, GI, GC)) for z in range(2)]
                    b = [b_raw[:, z].rearrange("p m (i c) -> p m i c", i=GI) for z in range(2)]
                    o = [bb[:, z].rearrange("p m (i c) -> p m i c", i=GI) for z in range(2)]
                    cmul(step, o, b, f, tmp_b[:, 0, 0:4 * GI * GC].rearrange("p (m i c) -> p m i c", m=4, i=GI))
                    step(*(V.tensor_copy(pr[:, :, s, :], pw[:, :, L - 1 - s, :]) for s in range(L)))
                    step(V.memset(hs[:, :, :, 0:1], 0.0))
                    V.memset(dtmp[:, 0, 0:1], 0.0).then_inc(bb_done.sem, 1)

                def index_acc(n):
                    b, h = n // IDX_HEADS + 1, n % IDX_HEADS
                    w = (b + 1) * P
                    wait(dve, idx_relu, l, n)
                    dst, w_h = score[b], wi_n[:, b, h:h + 1]
                    if h == 0:
                        i = V.tensor_scalar(dst, tmp_a[:, n % 2, 0:w], w_h, None, ALU.mult)
                    else:
                        i = V.scalar_tensor_tensor(out=dst, in0=tmp_a[:, n % 2, 0:w], scalar=w_h, in1=dst, op0=ALU.mult, op1=ALU.add)
                    i.then_inc(idx_acc.sem, 1)
                    wait(dve, idx_acc, l, n)

                def topk_start(b):
                    step(V.memset(score[b][0:64, (b + 1) * P - 64:(b + 1) * P], INADM))

                def topk_round(b):
                    s = score[b]
                    settle(dve)
                    step(V.max(top8[:], s))
                    settle(dve)
                    step(V.match_replace(out=s, in_to_replace=top8[:], in_values=s, imm_value=TAKEN))

                def topk_end(b):
                    s = score[b]
                    V.tensor_scalar(s, s, -3.2e38, NEG, ALU.is_gt, ALU.mult).then_inc(mask_done.sem, 1)
                    wait(dve, mask_done, l, b)

                def mask0():
                    step(V.memset(score[0], 0.0))
                    V.memset(score[0][0:64, 64:P], NEG).then_inc(mask_done.sem, 1)
                    wait(dve, mask_done, l, 0)

                def mask_head(e):
                    b = e // HEADS
                    w = (b + 1) * P
                    wait(dve, logit, l, e)
                    if e >= 2:
                        wait(dve, p_exp, l, e - 2)
                        wait(dve, masked, l, e - 1)
                    settle(dve)
                    V.tensor_tensor_reduce(tmp_a[:, e % 2, 0:w], ps[:, e % 2, 0:w], score[b], -ATT_SCALE, 3.4e38,
                                           ALU.add, ALU.min, nmax[:, e % 2:e % 2 + 1]).then_inc(masked.sem, 1)

                def att_step(b, i):
                    if i == 1:
                        wait(dve, pv, l, b * HEADS + HEADS - 1)
                        wait(dve, p_exp, l, b * HEADS + HEADS - 1)
                        if b:
                            wait(dve, att_tr, l, b - 1)
                        step(V.reciprocal(rinv[:], rsum[:, b % 2, :]))
                        V.tensor_tensor(att[:], ps[:, 3, :].rearrange("p (h d) -> p h d", d=HD),
                                        rinv[:].unsqueeze(2).broadcast_to((P, HEADS, HD)), ALU.mult).then_inc(att_n.sem, 1)
                    if i == 3:
                        wait(dve, att_sq, l, b)
                        V.tensor_scalar(att_ss[:, 1:2], att_ss[:, 0:1], 1.0 / SW, EPS, ALU.mult, ALU.add).then_inc(att_ms.sem, 1)
                    if i == 4:
                        wait(dve, att_rs, l, b)
                        V.tensor_scalar(att[:], att[:], att_ss[:, 2:3], None, ALU.mult).then_inc(att_sc.sem, 1)
                    if i == 6:
                        wait(dve, att_tr, l, b)
                        if b:
                            wait(dve, att_done, l, b - 1)
                        V.tensor_tensor(z_t[:, 1, :].rearrange("p (m t) -> p m t", m=AT),
                                        ps[:, 7, :].rearrange("p (m t) -> p m t", m=AT),
                                        vcols[:, ds(56 + AT * l, AT)].unsqueeze(2).broadcast_to((P, AT, P)), ALU.mult).then_inc(att_f.sem, 1)
                    if i == 8:
                        wait(dve, att_hi, l, b)
                        V.tensor_tensor(h_lo[:, 0:AT, b * P:(b + 1) * P], z_t[:, 1, :].rearrange("p (m t) -> p m t", m=AT),
                                        h_hi[:, 0:AT, b * P:(b + 1) * P].bitcast(F32), ALU.subtract).then_inc(att_done.sem, 1)

                def s5_d(m):
                    wait(dve, kk_copy, l, 2 * m + 1)
                    kk = kk_y[0:GC, :].rearrange("c (g n) -> c g n", g=2 * GI)[:, :, 0:GC]
                    step(V.tensor_tensor(dtmp[:], ident[0:GC, 0:GC].unsqueeze(1).broadcast_to((GC, 2 * GI, GC)),
                                         d_raw[:, 2 * GI * m:2 * GI * (m + 1)].unsqueeze(2).broadcast_to((GC, 2 * GI, GC)), ALU.mult))
                    V.tensor_tensor(kk, kk, dtmp[:], ALU.add).then_inc(kk_d.sem, 1)
                    wait(dve, kk_d, l, m)

                def s5_scan(m):
                    wait(dve, st_mm, l, m)
                    wait(dve, prep, l, 3 * m + 2)
                    S = [ps[:, 6, z * GI * J:(z + 1) * GI * J].rearrange("p (i j) -> p i j", i=GI) for z in range(2)]
                    E = [rot[:, m % 2, z] for z in range(2)]
                    X = [xr[:, z] for z in range(2)]
                    Gs = [gr[:, z] for z in range(2)]
                    M = [s5_m[:, z] for z in range(2)]
                    step(V.tensor_tensor(X[0], E[0], S[0], ALU.mult), V.tensor_tensor(M[0], E[1], S[1], ALU.mult),
                         V.tensor_tensor(X[1], E[0], S[1], ALU.mult), V.tensor_tensor(M[1], E[1], S[0], ALU.mult))
                    step(V.tensor_tensor(X[0], X[0], M[0], ALU.add), V.tensor_tensor(X[1], X[1], M[1], ALU.subtract))
                    flat = lambda v: v.rearrange("p i j -> p (i j)")
                    step(*(V.tensor_tensor_scan(flat(Gs[z]), flat(dec[:, m % 2]), flat(X[z]), 0.0, ALU.mult, ALU.add) for z in range(2)))
                    step(V.tensor_tensor(X[0], E[0], Gs[0], ALU.mult), V.tensor_tensor(M[0], E[1], Gs[1], ALU.mult),
                         V.tensor_tensor(X[1], E[0], Gs[1], ALU.mult), V.tensor_tensor(M[1], E[1], Gs[0], ALU.mult))
                    if m:
                        wait(dve, y_mm, l, m - 1)
                    step(V.tensor_tensor(hs[:, 0, :, 1:J + 1], X[0], M[0], ALU.subtract))
                    V.tensor_tensor(hs[:, 1, :, 1:J + 1], X[1], M[1], ALU.add).then_inc(hs_done.sem, 1)
                    wait(dve, hs_done, l, m)

                def s5_lo(m):
                    wait(dve, y_act, l, 2 * m + 1)
                    V.tensor_tensor(h_lo[:, AT + m, :], u_t[:, m].rearrange("p a b -> p (a b)"), h_hi[:, AT + m, :].bitcast(F32), ALU.subtract).then_inc(y_done.sem, 1)

                def s5_step(e):
                    m, h = divmod(e + S5_LEAD, HEADS)
                    if m < 4 and h == 2:
                        s5_d(m)
                    if m < 4 and h == 6:
                        s5_scan(m)

                for t in range(12):
                    split_lo(l, m0 + t + AHEAD)
                    if t == 2:
                        rope(0)
                    if t == 3:
                        rope(1)
                        b_bar()
                    if t == 4:
                        rope(2)
                        rope(3)
                        mask0()
                    if t >= 6 and t <= 9:
                        rope(t - 2)
                    if t == 6:
                        wait(dve, v_done, l, 1)
                    if t in (6, 7, 8):
                        for n in range(IDX_HEADS):
                            index_acc((t - 6) * IDX_HEADS + n)
                        topk_start(t - 5)
                    if t > 12 - S5_LEAD:
                        s5_step(t - 12)
                for n in range(2):
                    split_lo(l, m0 + 12 + n + AHEAD)
                for b in range(QB):
                    for h in range(HEADS):
                        mask_head(b * HEADS + h)
                        if b:
                            att_step(b - 1, h)
                        if b > 1 and h == 0:
                            att_step(b - 2, 8)
                        s5_step(b * HEADS + h)
                        if b < QB - 1:
                            topk_round(b + 1)
                            topk_round(b + 1)
                    if b < QB - 1:
                        topk_end(b + 1)
                att_step(QB - 1, 1)
                att_step(QB - 2, 8)
                att_step(QB - 1, 3)
                att_step(QB - 1, 4)
                for m in range(ST):
                    s5_lo(m)
                for n in range(ST):
                    wait(dve, glu_act, l, n)
                    V.scalar_tensor_tensor(out=q_t[:, n, :], in0=tmp_a[:, n % 2, :], scalar=1.0,
                                           in1=u_t[:, n].rearrange("p a b -> p (a b)"), op0=ALU.add, op1=ALU.mult).then_inc(ssm_y.sem, 1)
                    if n < 2:
                        split_lo(l, m0 + 14 + n + AHEAD)
                att_step(QB - 1, 6)
                att_step(QB - 1, 8)
                wait(dve, ssm_ss, l, ST - 1)
                rms(l, 2, 4 * SW, step)
                wait(dve, bcast, l, 2)
                wait(dve, ssm_y, l, ST - 1)
                for n in range(ST):
                    if n >= 2:
                        wait(dve, mix_done, l, n - 2)
                    V.scalar_tensor_tensor(out=tmp_a[:, n % 2, :], in0=q_t[:, n, :], scalar=half_gain[:, n:n + 1],
                                           in1=ps[:, 7, :], op0=ALU.mult, op1=ALU.mult).then_inc(ssm_f.sem, 1)
                    wait(dve, ssm_hi, l, n)
                    V.tensor_tensor(h_lo[:, AT + n, :], tmp_a[:, n % 2, :], h_hi[:, AT + n, :].bitcast(F32), ALU.subtract).then_inc(mix_done.sem, 1)
                for n in range(KT):
                    split_lo(l, m0 + 16 + n + AHEAD)
                    if n:
                        add_squares(l, KT + n - 1)
                    update(l, 1, n)
                add_squares(l, KT + KT - 1)

            steps = [0]
            with dve.Fori(0, DEPTH) as l:
                steps[0] = 0

                def chain():
                    c = Chain(dve, dve_step, l, DVE_STEPS)
                    c.n = steps[0]
                    return c

                step = chain()
                norm(l, 0, 0, 1, 0, 2, 0.5, step)
                steps[0] = step.n
                ffn_dve(l, 0)
                step = chain()
                step(gates(l, 1, 5, 1.0), V.tensor_scalar(half_bias[:], vcols[:, ds(72 + ST * l, ST)], 0.5, None, ALU.mult),
                     V.tensor_scalar(half_gain[:], vcols[:, ds(64 + ST * l, ST)], 0.5, None, ALU.mult))
                norm(l, 1, 1, 4, 3, 5, 1.0, step)
                mixer_dve(l, step)
                norm(l, 2, 3, 7, 6, 8, 0.5, step)
                steps[0] = step.n
                ffn_dve(l, 1)
                assert steps[0] == DVE_STEPS, steps[0]

            wait(dve, ssq, DEPTH, -1)
            rms(DEPTH, 0, D, None)
            wait(dve, bcast, DEPTH, 0)
            for n in range(KT):
                if n >= 2:
                    dve.wait_ge(out_tr, n - 1)
                V.scalar_tensor_tensor(out=o_t[:, n % 2, :], in0=x[:, n, :], scalar=vcols[:, 48 + n:49 + n], in1=ps[:, 7, :],
                                       op0=ALU.mult, op1=ALU.mult).then_inc(out_f, 1)

        @block.gpsimd
        def _(pool):
            Q = nc.gpsimd

            def power(layer, idx):
                wait(pool, ms_ready, layer, idx)
                Q.tensor_tensor(rstd[:], ms[:], mhalf[:], ALU.pow).then_inc(rstd_ready.sem, 1)

            def cmul(step, o, p, q, t, p0n=None):
                step(Q.tensor_tensor(o[0], p[0], q[0], ALU.mult), Q.tensor_tensor(t, p[1], q[1], ALU.mult))
                step(Q.tensor_tensor(o[0], o[0], t, ALU.subtract))
                step(Q.tensor_tensor(o[1], p[0] if p0n is None else p0n, q[1], ALU.mult), Q.tensor_tensor(t, p[1], q[0], ALU.mult))
                step(Q.tensor_tensor(o[1], o[1], t, ALU.add if p0n is None else ALU.subtract))

            def ready(l, event, step):
                settle(pool)
                Q.memset(pool_t[:, 0:1], 0.0).then_inc(prep.sem, 1)
                wait(pool, prep, l, event)

            def s5_ca(l, m, step):
                if m >= 2:
                    wait(pool, y_mm, l, m - 2)
                n9 = (P, GI, L + 1, GC)
                c3 = [ct[:, z, m, :].rearrange("p (i c) -> p i c", i=GI).unsqueeze(2).broadcast_to(n9) for z in range(3)]
                q9 = [pw[:, z, :, m * GI:(m + 1) * GI].rearrange("p t i -> p i t").unsqueeze(3).broadcast_to(n9) for z in range(2)]
                cmul(step, [ca[:, m % 2, z] for z in range(2)], c3[0:2], q9,
                     pool_t[:].rearrange("p (i t c) -> p i t c", i=GI, c=GC), p0n=c3[2])
                ready(l, 3 * m, step)

            def s5_ab(l, m, step):
                n8 = (P, GI, L, GC)
                b2 = [bb[:, z, m, :].rearrange("p (i c) -> p i c", i=GI).unsqueeze(2).broadcast_to(n8) for z in range(2)]
                q8 = [pr[:, z, :, m * GI:(m + 1) * GI].rearrange("p t i -> p i t").unsqueeze(3).broadcast_to(n8) for z in range(2)]
                cmul(step, [ab[m % 2][:, z] for z in range(2)], b2, q8,
                     pool_t[:, 0:GI * L * GC].rearrange("p (i t c) -> p i t c", i=GI, c=GC))
                ready(l, 3 * m + 1, step)

            def s5_rot(l, m, step):
                r = [rot[:, m % 2, z] for z in range(2)]
                settle(pool)
                step(Q.memset(r[0][:, :, 0:1], 1.0), Q.memset(r[1][:, :, 0:1], 0.0),
                     Q.memset(dec[:, m % 2, :, 0:1], 0.0),
                     Q.tensor_copy(dec[:, m % 2, :, 1:J], mag_l[:, m * GI:(m + 1) * GI].unsqueeze(2).broadcast_to((P, GI, J - 1))))
                for k in range(6):
                    n = 1 << k
                    e = [en[:, z, k, m * GI:(m + 1) * GI].unsqueeze(2).broadcast_to((P, GI, n)) for z in range(2)]
                    cmul(step, [r[z][:, :, n:2 * n] for z in range(2)], [r[z][:, :, 0:n] for z in range(2)], e,
                         pool_t[:, 0:GI * n].rearrange("p (i j) -> p i j", i=GI))
                ready(l, 3 * m + 2, step)

            pool.wait_ge(credits, 3)
            with pool.Fori(0, DEPTH) as l:
                step = Chain(pool, pool_step, l, POOL_STEPS)
                power(l, 0)
                power(l, 1)
                projected(pool, l, KT - 1)
                settle(pool)
                Q.memset(toep[:], 0.0).then_inc(toep0.sem, 1)
                wait(pool, ct_done, l, 2)
                wait(pool, bb_done, l, 0)

                def att_power(b):
                    wait(pool, att_ms, l, b)
                    Q.tensor_tensor(att_ss[:, 2:3], att_ss[:, 1:2], mhalf[:, 0:1], ALU.pow).then_inc(att_rs.sem, 1)

                for m in range(4):
                    s5_ca(l, m, step)
                    s5_ab(l, m, step)
                    if m >= 2:
                        att_power(m - 2)
                    s5_rot(l, m, step)
                att_power(2)
                att_power(3)
                power(l, 2)
                power(l, 3)
                assert step.n == POOL_STEPS, step.n
            power(DEPTH, 0)

        @block.tensor
        def _(pe):
            mm = nc.tensor.matmul

            def split3(out, w, rhs_hi, rhs_lo, first, last):
                hi, lo = w
                mm(out, hi, rhs_hi, start=first, stop=False)
                mm(out, hi, rhs_lo, start=False, stop=False)
                return mm(out, lo, rhs_hi, start=False, stop=last)

            def w_tile(c, k):
                s = slice(k * P, (k + 1) * P)
                return w_hi[:, c % RING, s], w_lo[:, c % RING, s]

            def chunk_ready(layer, c, shift=0):
                pe.wait_ge(w_split_lo.sem, w_split_lo.after(layer, c) + shift)

            def mod_sum(layer, j, turn=0):
                pe.wait_ge(acc_ready.sem, acc_ready.after(layer, j) + turn)
                pe.wait_ge(mod_done.sem, mod_done.after(layer, j - 1) + turn)
                for k in range(KT):
                    i = mm(ps[:, 7, k:k + 1], mod_acc[:, k * P:(k + 1) * P], ones[:, 0:1], start=True, stop=True)
                i.then_inc(mod_psum.sem, 1)

            def feature_sums(layer, k3):
                wait(pe, sq_sum, layer, (k3 + 1) * (KT - 1) - 1)
                for b in range(QB):
                    i = mm(ps[:, 6, b:b + 1], tmp_a[:, 0, b * P:(b + 1) * P], ones[:, 0:1], start=True, stop=True)
                i.then_inc(ssq.sem, 1)

            def squares_sum(layer, e, buf, done, src, last_k, k):
                wait(pe, done, layer, e)
                for b in range(QB):
                    i = mm(ps[:, 6, b:b + 1], tmp_b[:, buf, b * P:(b + 1) * P], ones[:, 0:1],
                           start=(k == 0 and b == 0), stop=(k == last_k), skip_group_check=True)
                i.then_inc(src.sem, 1)

            def rms_bcast(layer, idx):
                wait(pe, diag_ready, layer, idx)
                mm(ps[:, 7, :], ones[:], tmp_b[:, 0, :], start=True, stop=True).then_inc(bcast.sem, 1)

            pe.wait_ge(in_const, 32)
            pe.wait_ge(in_c, 96)
            nc.tensor.transpose(ps[:, 4, 0:88], vraw[0:88, 0, :], ident[0:88, 0:88]).then_inc(prologue, 1)
            pe.wait_ge(in_vec, 32)
            for l in range(DEPTH):
                nc.tensor.transpose(ps[:, 5, l * P:l * P + 72], vraw[0:72, 1 + l, :], ident[0:72, 0:72]).then_inc(prologue, 1)
            pe.wait_ge(credits, 6)
            pe.wait_ge(in_x, 16)
            for n in range(KT):
                wait(pe, x_new, 0, n - KT - 2)
                for b in range(QB):
                    i = nc.tensor.transpose(ps[:, 4 + n % 2, b * P:(b + 1) * P], x_in[:, b, n * P:(n + 1) * P], ident[:])
                i.then_inc(prologue, 1)
            feature_sums(0, -1)
            for j in range(2):
                pe.wait_ge(acc_ready.sem, j + 1)
                if j:
                    pe.wait_ge(mod_done.sem, j)
                for k in range(KT):
                    i = mm(ps[:, 7, k:k + 1], (mod_acc, mod_acc_b)[j][:, k * P:(k + 1) * P], ones[:, 0:1], start=True, stop=True)
                i.then_inc(mod_psum.sem, 1)

            def ffn_pe(l, ffn):
                c0, f0 = FFN_BASE[ffn], ffn * FT

                rms_bcast(l, 3 * ffn)
                if ffn == 0:
                    s5_select(l)
                with pe.Fori(0, A_TURNS) as i:
                    for u in range(A_UNROLL):
                        tile_pe(l, ffn, u, u % 2, A_UNROLL * i, 2 * A_UNROLL * i, u == 0)
                    if ffn == 0:
                        mod_sum(l, 0, turn=i)
                for f in (FT - 2, FT - 1):
                    tile_pe(l, ffn, f, f % 2, 0, 0, False)
                mod_sum(l, A_TURNS + ffn)
                wait(pe, g_done, l, f0 + FT - 1)
                for n in range(KT):
                    e = 2 * ffn * KT + n
                    if n < KT:
                        wait(pe, x_new, l, e - 2)
                        for j in range(3):
                            c = c0 + 2 * FT + 3 * n + j
                            chunk_ready(l, c)
                            k0, kn = down_chunk(j)
                            for k in range(kn):
                                i = split3(ps[:, 4 + n % 2, :], w_tile(c, k), g_hi[:, k0 + k, :], g_lo[:, k0 + k, :],
                                           k0 + k == 0, k0 + k == FT - 1)
                            i.then_inc(w_used.sem, 1)
                        if ffn == 1 and n % 4 == 3:
                            mod_sum(l, A_TURNS + 2 + n // 4)
                feature_sums(l, 2 * ffn)

            def tile_pe(l, ffn, f, parity, shift, cshift, by_k):
                c, f0 = FFN_BASE[ffn] + 2 * f, ffn * FT
                pe.wait_ge(w_split_lo.sem, w_split_lo.after(l, c + 1) + cshift)
                pe.wait_ge(g_full.sem, g_full.after(l, f0 + f - 2) + shift)
                for k in range(KT):
                    if by_k:
                        wait(pe, h_done, l, 2 * ffn * KT + k)
                    for z in range(2):
                        i = split3(ps[:, 2 * parity + z, :], w_tile(c + z, k), h_hi[:, k, :], h_lo[:, k, :], k == 0, k == KT - 1)
                        if k == KT - 1:
                            i.then_inc(w_used.sem, 1)

            def s5_select(l):
                pe.wait_ge(s5_in.sem, 64 * l + 64)
                sel = ident[0:G, 0:G].rearrange("g (m t i) -> g t m i", t=2, i=GI)
                for z in range(2):
                    for g2 in range(2):
                        i = mm(ps[g2 * NS:(g2 + 1) * NS, 6, 16 + z * NQ:16 + (z + 1) * NQ], s5_raw[:, z, :], sel[:, g2],
                               start=True, stop=True)
                i.then_inc(s5_sel.sem, 1)

            def mixer_pe(l):
                m0 = MIX_BASE

                def project(t):
                    c = m0 + t
                    chunk_ready(l, c)
                    if t >= 2:
                        wait(pe, z_copy, l, t - 2)
                    for k in range(KT):
                        if t == 0:
                            wait(pe, h_done, l, KT + k)
                        i = split3(ps[:, t % 2, :], w_tile(c, k), h_hi[:, k, :], h_lo[:, k, :], k == 0, k == KT - 1)
                    i.then_inc(w_used.sem, 1)

                def swap(r, t, first, second):
                    wait(pe, z_copy, l, t)
                    if r:
                        wait(pe, rope_done, l, r - 1)
                    if first is not None:
                        mm(ps[:, 2, :], swaps[:, first, :], z_t[:, t % 2, :], start=True, stop=True)
                    mm(ps[:, 3, :], swaps[:, second, :], z_t[:, t % 2, :], start=True, stop=True).then_inc(swap_mm.sem, 1)

                def index(n):
                    b, h = n // IDX_HEADS + 1, n % IDX_HEADS
                    r = slice(h % 2 * HD, h % 2 * HD + HD)
                    if n >= 2:
                        wait(pe, idx_relu, l, n - 2)
                    mm(ps[:, 4 + n % 2, 0:(b + 1) * P], qi_t[r, h // 2, b * P:(b + 1) * P], ki_t[r, 0:(b + 1) * P],
                       start=True, stop=True).then_inc(idx_mm.sem, 1)

                def logits(e):
                    b, h = e // HEADS, e % HEADS
                    r = slice(h % 2 * HD, h % 2 * HD + HD)
                    if e >= 2:
                        wait(pe, masked, l, e - 2)
                    mm(ps[:, e % 2, 0:(b + 1) * P], q_t[r, h // 2, b * P:(b + 1) * P], k_t[r, 0:(b + 1) * P],
                       start=True, stop=True).then_inc(logit.sem, 1)

                def turn(e):
                    b = e // HEADS
                    wait(pe, p_exp, l, e)
                    if e:
                        wait(pe, pt_copy, l, e - 1)
                    for s in range(b + 1):
                        i = nc.tensor.transpose(ps[:, 2, s * P:(s + 1) * P], tmp_b[:, e % 2, s * P:(s + 1) * P], ident[:])
                    i.then_inc(pt_mm.sem, 1)

                def values(e):
                    b, h = e // HEADS, e % HEADS
                    wait(pe, pt_copy, l, e)
                    if h == 0 and b:
                        wait(pe, att_n, l, b - 1)
                    for s in range(b + 1):
                        i = mm(ps[:, 3, h * HD:(h + 1) * HD], pt[:, e % 2, s * P:(s + 1) * P], v_n[:, s, :],
                               start=(s == 0), stop=(s == b))
                    i.then_inc(pv.sem, 1)

                def att_turn(b):
                    wait(pe, att_sc, l, b)
                    if b:
                        wait(pe, att_f, l, b - 1)
                    for m in range(AT):
                        i = nc.tensor.transpose(ps[:, 7, m * P:(m + 1) * P], att[:, 2 * m:2 * m + 2, :].rearrange("p h d -> p (h d)"), ident[:])
                    i.then_inc(att_tr.sem, 1)

                def halves(g):
                    return slice(g // GI * NS, (g // GI + 1) * NS), g % GI

                def s5_kk(m):
                    wait(pe, prep, l, 3 * m)
                    if m:
                        wait(pe, y_copy, l, 2 * m - 1)
                    settle(pe)
                    for g in range(2 * GI):
                        r, q = halves(g)
                        for z in range(2):
                            i = mm(ps[0:GC, 4 + g // GI, (g % GI) * P:(g % GI + 1) * P], bb[r, z, m, q * GC:(q + 1) * GC],
                                   ca[r, m % 2, z, q, 0:L, :].rearrange("p t c -> p (t c)"), start=(z == 0), stop=(z == 1))
                    i.then_inc(kk_mm.sem, 1)

                def s5_w(m):
                    wait(pe, kk_copy, l, 2 * m + 1)
                    wait(pe, prep, l, 3 * m + 1)
                    for z in range(2):
                        for q in range(GI):
                            i = nc.tensor.transpose(ps[:, 4 + z, q * P:(q + 1) * P], ab[m % 2][:, z, q].rearrange("p s c -> p (s c)"), ident[:])
                    i.then_inc(w_tr.sem, 1)

                def s5_un(m):
                    wait(pe, w_copy, l, 2 * m + 1)
                    settle(pe)
                    for s in range(L):
                        i = nc.tensor.transpose(ps[0:J, 4 + s // 4, (s % 4) * P:(s % 4 + 1) * P], u_t[:, m, s, :], ident[:])
                    i.then_inc(un_tr.sem, 1)

                def s5_u8(m):
                    wait(pe, un_copy, l, 2 * m + 1)
                    settle(pe)
                    for g in range(2 * GI):
                        i = nc.tensor.transpose(ps[:, 4, g * J:(g + 1) * J], un[:, g].rearrange("j s c -> j (s c)"), ident[0:J, 0:J])
                    i.then_inc(u8_tr.sem, 1)

                def s5_states(m):
                    wait(pe, u8_copy, l, m)
                    if m:
                        wait(pe, y_tile, l, m - 1)
                    for z in range(2):
                        for g in range(2 * GI):
                            r, q = halves(g)
                            i = mm(ps[r, 6, (z * GI + q) * J:(z * GI + q + 1) * J], wst[:, z, q, r], u8[:, g, :], start=True, stop=True)
                    i.then_inc(st_mm.sem, 1)

                def s5_y(m):
                    pe.wait_ge(toep_in.sem, toep_in.per * l + 16 * L * (m + 1))
                    wait(pe, hs_done, l, m)
                    for g in range(2 * GI):
                        r, q = halves(g)
                        out = ps[0:J, 4 + g // GI, (g % GI) * P:(g % GI + 1) * P]
                        mm(out, u8[:, g, :], toep[:, g, :], start=True, stop=False)
                        for z in range(2):
                            i = mm(out, hs[r, z, q, 0:J], ca[r, m % 2, z, q, 1:L + 1, :].rearrange("p t c -> p (t c)"),
                                   start=False, stop=(z == 1))
                    i.then_inc(y_mm.sem, 1)

                def s5_yt(m):
                    wait(pe, y_copy, l, 2 * m + 1)
                    settle(pe)
                    for t in range(L):
                        i = nc.tensor.transpose(ps[:, 6, t * J:(t + 1) * J], kk_y[:, t * P:(t + 1) * P], ident[0:J, 0:J])
                    i.then_inc(y_tr.sem, 1)

                def s5_step(e):
                    m, h = divmod(e + S5_LEAD, HEADS)
                    if h == 0 and m:
                        s5_yt(m - 1)
                    if m < 4 and h in (1, 2, 3, 4, 5, 7):
                        {1: s5_kk, 2: s5_w, 3: s5_un, 4: s5_u8, 5: s5_states, 7: s5_y}[h](m)

                rms_bcast(l, 1)
                for t in range(12):
                    project(t)
                    if t == 1:
                        pe.wait_ge(mix_in.sem, mix_in.per * (l + 1))
                        settle(pe)
                        for z in range(2):
                            for m in range(4):
                                i = nc.tensor.transpose(ps[:, 7, z * 256 + m * 64:z * 256 + (m + 1) * 64], c_raw[:, z, m, :], ident[0:64, 0:64])
                        i.then_inc(ct_mm.sem, 1)
                    if t in (1, 2):
                        swap(t - 1, t - 1, None, 0)
                    if t == 3:
                        swap(2, 2, 3, 4)
                        swap(3, 2, 1, 2)
                    if t == 4:
                        wait(pe, z_copy, l, 3)
                        for b in range(QB):
                            i = nc.tensor.transpose(ps[:, 4, b * P:(b + 1) * P], z_t[:, 1, b * P:(b + 1) * P], ident[:])
                        i.then_inc(v_tr.sem, 1)
                    if 5 <= t <= 8:
                        swap(t - 1, t - 1, None, 0)
                    if t == 6:
                        wait(pe, v_done, l, 1)
                        wait(pe, rope_done, l, 3)
                    if t in (6, 7, 8):
                        for n in range(IDX_HEADS):
                            index((t - 6) * IDX_HEADS + n)
                    if t > 12 - S5_LEAD:
                        wait(pe, idx_relu, l, 11)
                        s5_step(t - 12)
                wait(pe, z_copy, l, 11)
                wait(pe, idx_relu, l, 11)
                wait(pe, rope_done, l, 7)
                logits(0)
                for b in range(QB):
                    for h in range(HEADS):
                        e = b * HEADS + h
                        if e + 1 < NA:
                            logits(e + 1)
                        s5_step(e)
                        if h == 5 and b:
                            att_turn(b - 1)
                        turn(e)
                        if e:
                            values(e - 1)
                values(NA - 1)
                wait(pe, att_n, l, QB - 1)
                for n in range(ST):
                    c = m0 + 12 + n
                    chunk_ready(l, c)
                    for k in range(ST):
                        if n == 0:
                            wait(pe, y_done, l, k)
                        i = split3(ps[:, n, :], w_tile(c, k), h_hi[:, AT + k, :], h_lo[:, AT + k, :], k == 0, k == ST - 1)
                    i.then_inc(w_used.sem, 1)
                att_turn(QB - 1)
                for n in range(ST):
                    squares_sum(l, n, n % 2, ssm_sq, ssm_ss, ST - 1, n)
                rms_bcast(l, 2)
                wait(pe, att_done, l, QB - 1)
                for n in range(KT):
                    if n < KT:
                        c = m0 + 16 + n
                        chunk_ready(l, c)
                        wait(pe, x_new, l, KT + n - 2)
                        for k in range(KT):
                            if n == 0 and k >= AT:
                                wait(pe, mix_done, l, k - AT)
                            i = split3(ps[:, 4 + n % 2, :], w_tile(c, k), h_hi[:, k, :], h_lo[:, k, :], k == 0, k == KT - 1)
                        i.then_inc(w_used.sem, 1)
                feature_sums(l, 1)

            with pe.Fori(0, DEPTH) as l:
                ffn_pe(l, 0)
                mixer_pe(l)
                ffn_pe(l, 1)

            rms_bcast(DEPTH, 0)
            for n in range(KT):
                pe.wait_ge(out_f, n + 1)
                if n >= 2:
                    pe.wait_ge(out_copy, n - 1)
                for b in range(QB):
                    i = nc.tensor.transpose(ps[:, 4 + n % 2, b * P:(b + 1) * P], o_t[:, n % 2, b * P:(b + 1) * P], ident[:])
                i.then_inc(out_tr, 1)



_INS = ["x", "c", "positions", "mod_w", "mod_b", "norm_g", "ffn1_w1", "ffn1_w3", "ffn1_w2", "ffn2_w1", "ffn2_w3",
        "ffn2_w2", "w_in", "w_out", "attn_gain", "ssm_gain", "ssm_a_re", "ssm_a_im", "ssm_log_dt", "ssm_b_re",
        "ssm_b_im", "ssm_c_re", "ssm_c_im", "ssm_d", "glu_w", "glu_b", "final_g"]


def kernel(**inputs):
    import concourse.bacc as bacc
    from concourse.bass_utils import run_bass_kernel_spmd

    nc = bacc.Bacc("TRN2", target_bir_lowering=False, num_devices=1, dynamic_dma_scratch_size=1024)
    arrays = {f"in_{n}": np.ascontiguousarray(inputs[n]) for n in _INS}
    arrays["in_consts"] = shape_constants()
    a = {n[3:]: nc.dram_tensor(n, v.shape, mybir.dt.from_np(v.dtype), kind="ExternalInput").ap() for n, v in arrays.items()}
    a["out"] = nc.dram_tensor("out", (1, SEQ, D), F32, kind="ExternalOutput").ap()
    trunk(nc, a)
    r = run_bass_kernel_spmd(nc, [arrays], core_ids=[0])
    return r.results[0]["out"]
```
